# Optimizing a Trainium2 kernel written in Bass

```python
import jax, jax.numpy as jnp
from jax import lax
import numpy as np

D_MODEL = 2048
BATCH = 1
SEQ = 512
DEPTH = 1

N_META = 16
D_MIX = D_MODEL
D_CONV = D_MIX // 2
D_RWKV = D_MIX - D_CONV
HEAD_SIZE = 64
N_CONV_GROUPS = D_CONV // HEAD_SIZE
N_RWKV_HEADS = D_RWKV // HEAD_SIZE
CONV_WIDTH = 3
R_DECAY = 64
R_AAA = 64
R_MV = 32
R_GATE = 160
D_FF = 4 * D_MODEL
NORM_EPS = 1e-5
LNX_EPS = 1e-5 * HEAD_SIZE
L2_EPS = 1e-12
N_CONV_COLS = 3 * D_CONV
N_RWKV_COLS = 3 * D_RWKV + R_DECAY + R_AAA + R_GATE
N_IN_COLS = N_CONV_COLS + N_RWKV_COLS

kernel_name = "hybrid_shortconv_rwkv7_meta"

def rms_norm(x, g):
    xf = x.astype(jnp.float32)
    y = xf * lax.rsqrt(jnp.mean(xf * xf, axis=-1, keepdims=True) + NORM_EPS)
    return (y * g.astype(jnp.float32)).astype(x.dtype)

def token_shift(p, mu):
    prev = jnp.pad(p[:, :-1], ((0, 0), (1, 0), (0, 0)))
    return p + (prev - p) * mu

def short_conv_group(p_conv, conv_w):
    xc, b_gate, c_gate = jnp.split(p_conv, 3, axis=-1)
    u = c_gate * xc
    L = u.shape[1]
    u_pad = jnp.pad(u, ((0, 0), (CONV_WIDTH - 1, 0), (0, 0)))
    conv = sum(conv_w[j] * u_pad[:, j:j + L] for j in range(CONV_WIDTH))
    return b_gate * conv

def wkv7_scan(r, decay, k, v, a_, b_):
    xs = tuple(jnp.moveaxis(t, 1, 0) for t in (r, decay, k, v, a_, b_))
    B, _, H, N = r.shape

    def step(S, inp):
        r_t, w_t, k_t, v_t, a_t, b_t = inp
        sa = jnp.einsum('bhij,bhj->bhi', S, a_t)
        S = (S * w_t[:, :, None, :] + sa[..., :, None] * b_t[:, :, None, :]
             + v_t[..., :, None] * k_t[:, :, None, :])
        y = jnp.einsum('bhij,bhj->bhi', S, r_t)
        return S, y

    S0 = jnp.zeros((B, H, N, N), jnp.float32)
    _, ys = lax.scan(step, S0, xs)
    return jnp.moveaxis(ys, 0, 1)

def rwkv7_group(z, v_first, w0, w2, a0, a2, g2, k_k, k_a, r_k, lnx_w, lnx_b,
                v0=None, v2=None):
    B, L, _ = z.shape
    dt = z.dtype
    zf = z.astype(jnp.float32)
    o = 0
    r = zf[..., o:o + D_RWKV]; o += D_RWKV
    k = zf[..., o:o + D_RWKV]; o += D_RWKV
    v = zf[..., o:o + D_RWKV]; o += D_RWKV
    wd = zf[..., o:o + R_DECAY]; o += R_DECAY
    ad = zf[..., o:o + R_AAA]; o += R_AAA
    gd = zf[..., o:o + R_GATE]; o += R_GATE
    f32 = lambda t: t.astype(jnp.float32)
    w = -jax.nn.softplus(-(f32(w0) + jnp.tanh(wd) @ f32(w2))) - 0.5
    decay = jnp.exp(-jnp.exp(w))
    a = jax.nn.sigmoid(f32(a0) + ad @ f32(a2))
    g = jax.nn.sigmoid(gd) @ f32(g2)
    if v0 is None:
        v_first = v
    else:
        vd = zf[..., o:o + R_MV]
        v = v + (v_first - v) * jax.nn.sigmoid(f32(v0) + vd @ f32(v2))
    kk = k * f32(k_k)
    heads = lambda t: t.reshape(B, L, N_RWKV_HEADS, HEAD_SIZE)
    kk = heads(kk)
    kk = kk / jnp.maximum(jnp.linalg.norm(kk, axis=-1, keepdims=True), L2_EPS)
    k = k * (1.0 + (a - 1.0) * f32(k_a))
    rh, kh, vh, ah = heads(r), heads(k), heads(v), heads(a)
    y = wkv7_scan(rh, heads(decay), kh, vh, -kk, kk * ah)
    mean = jnp.mean(y, axis=-1, keepdims=True)
    var = jnp.mean(jnp.square(y - mean), axis=-1, keepdims=True)
    y = (y - mean) * lax.rsqrt(var + LNX_EPS)
    y = y.reshape(B, L, D_RWKV) * f32(lnx_w) + f32(lnx_b)
    bonus = jnp.sum(rh * kh * f32(r_k), axis=-1, keepdims=True) * vh
    y = (y + bonus.reshape(B, L, D_RWKV)) * g
    return y.astype(dt), v_first

def setup_inputs(seed: int = 0) -> dict:
    key = jax.random.key(seed)
    ks = jax.random.split(key, 32)
    nrm = lambda k, s, sc: jax.random.normal(k, s, jnp.float32) * sc
    Dm1 = DEPTH - 1
    decay_base = jnp.linspace(-6.0, 1.0, D_RWKV, dtype=jnp.float32)
    return {
        "x": nrm(ks[0], (BATCH, SEQ, D_MODEL), 1.0),
        "meta_tokens": nrm(ks[1], (N_META, D_MODEL), 1.0),
        "norm_mix_g": 1.0 + nrm(ks[2], (DEPTH, D_MODEL), 0.02),
        "w_in": nrm(ks[3], (DEPTH, D_MODEL, N_IN_COLS), D_MODEL ** -0.5),
        "w_in_vres": nrm(ks[4], (Dm1, D_MODEL, R_MV), D_MODEL ** -0.5),
        "shift_mu": jax.random.uniform(ks[5], (DEPTH, N_RWKV_COLS), jnp.float32),
        "shift_mu_vres": jax.random.uniform(ks[6], (Dm1, R_MV), jnp.float32),
        "conv_w": nrm(ks[7], (DEPTH, CONV_WIDTH, D_CONV), CONV_WIDTH ** -0.5),
        "decay_w0": decay_base + nrm(ks[8], (DEPTH, D_RWKV), 0.1),
        "decay_w2": nrm(ks[9], (DEPTH, R_DECAY, D_RWKV), 0.5 * R_DECAY ** -0.5),
        "iclr_a0": nrm(ks[10], (DEPTH, D_RWKV), 0.1),
        "iclr_a2": nrm(ks[11], (DEPTH, R_AAA, D_RWKV), 0.5 * R_AAA ** -0.5),
        "gate_g2": nrm(ks[12], (DEPTH, R_GATE, D_RWKV), R_GATE ** -0.5),
        "k_k": 0.85 + nrm(ks[13], (DEPTH, D_RWKV), 0.02),
        "k_a": 1.0 + nrm(ks[14], (DEPTH, D_RWKV), 0.02),
        "r_k": nrm(ks[15], (DEPTH, N_RWKV_HEADS, HEAD_SIZE), 0.1),
        "lnx_w": 1.0 + nrm(ks[16], (DEPTH, D_RWKV), 0.02),
        "lnx_b": nrm(ks[17], (DEPTH, D_RWKV), 0.02),
        "vres_v0": nrm(ks[18], (Dm1, D_RWKV), 0.1),
        "vres_v2": nrm(ks[19], (Dm1, R_MV, D_RWKV), 0.5 * R_MV ** -0.5),
        "w_out": nrm(ks[20], (DEPTH, D_MIX, D_MODEL), D_MIX ** -0.5),
        "norm_mlp_g": 1.0 + nrm(ks[21], (DEPTH, D_MODEL), 0.02),
        "w_up": nrm(ks[22], (DEPTH, D_MODEL, D_FF), D_MODEL ** -0.5),
        "w_down": nrm(ks[23], (DEPTH, D_FF, D_MODEL), D_FF ** -0.5),
        "final_norm_g": 1.0 + nrm(ks[24], (D_MODEL,), 0.02),
    }

def reference(x, meta_tokens, norm_mix_g, w_in, w_in_vres, shift_mu, shift_mu_vres,
              conv_w, decay_w0, decay_w2, iclr_a0, iclr_a2, gate_g2, k_k, k_a, r_k,
              lnx_w, lnx_b, vres_v0, vres_v2, w_out, norm_mlp_g, w_up, w_down,
              final_norm_g):
    B = x.shape[0]
    meta = jnp.broadcast_to(meta_tokens.astype(x.dtype)[None], (B, N_META, D_MODEL))
    h_res = jnp.concatenate([meta, x], axis=1)
    v_first = None
    for i in range(DEPTH):
        h = rms_norm(h_res, norm_mix_g[i])
        if i == 0:
            w_cat, mu = w_in[i], shift_mu[i]
        else:
            w_cat = jnp.concatenate([w_in[i], w_in_vres[i - 1]], axis=1)
            mu = jnp.concatenate([shift_mu[i], shift_mu_vres[i - 1]], axis=0)
        p = h @ w_cat
        y_conv = short_conv_group(p[..., :N_CONV_COLS], conv_w[i])
        z = token_shift(p[..., N_CONV_COLS:], mu)
        if i == 0:
            y_rwkv, v_first = rwkv7_group(
                z, None, decay_w0[i], decay_w2[i], iclr_a0[i], iclr_a2[i], gate_g2[i],
                k_k[i], k_a[i], r_k[i], lnx_w[i], lnx_b[i])
        else:
            y_rwkv, _ = rwkv7_group(
                z, v_first, decay_w0[i], decay_w2[i], iclr_a0[i], iclr_a2[i], gate_g2[i],
                k_k[i], k_a[i], r_k[i], lnx_w[i], lnx_b[i],
                vres_v0[i - 1], vres_v2[i - 1])
        y = jnp.concatenate([y_conv, y_rwkv], axis=-1) @ w_out[i]
        h_res = h_res + y
        h = rms_norm(h_res, norm_mlp_g[i])
        h_res = h_res + jnp.square(jax.nn.relu(h @ w_up[i])) @ w_down[i]
    out = rms_norm(h_res, final_norm_g)
    return out[:, N_META:]


_drawn_inputs = setup_inputs


def setup_inputs(seed=0):
    import zlib

    import numpy as np

    out = dict(_drawn_inputs(seed))
    spreads = {}
    factors = {'decay_w2': 3.797,
     'iclr_a0': 3.665,
     'k_k': 36.543,
     'k_a': 7.669,
     'lnx_w': 8.0,
     'lnx_b': 22.552,
     'norm_mlp_g': 3.459,
     'final_norm_g': 8.086}
    for name, (base, spread) in spreads.items():
        noise = np.random.default_rng([zlib.crc32(name.encode()), seed]).standard_normal(out[name].shape)
        drawn = base * np.exp(spread * noise) if base else spread * noise
        out[name] = __import__('jax').numpy.asarray(drawn.astype(out[name].dtype))
    for name, factor in factors.items():
        out[name] = (out[name] * factor).astype(out[name].dtype)
    return out
```

```python
import math
from contextlib import ExitStack

import concourse.bass as bass
from concourse import mybir

F32 = mybir.dt.float32
F32R = mybir.dt.float32r
ALU = mybir.AluOpType
ACT = mybir.ActivationFunctionType

P = 128
D = 2048
KT = D // P
META = 16
SEQ = 512
T = META + SEQ
HALF = T // 2
DH = D // 2
PAIRS = DH // P
HS = 64
CONV = 3 * DH
LOWR = 2 * DH * 3
GATE_TAIL = 32
DFF = 4 * D
C = 88
NCH = T // C
CP = 96
MID = C // 2 - 1
LEVELS = [1, 2, 4, 8, 16, 32, 64]
NORM_EPS = 1e-5
LNX_EPS = 1e-5 * HS
KQ = 4
RAW = 4
RING = 8
LEAD = 4
FFG = DFF // 1024
UT = 1024 // P

PE_STEPS = (["ss", "low", "vtr", "bsum", "atr", "btr", "ktr", "gram0", "gram1", "gram2", "mv", "x1"]
            + [f"{s}{m}{h}" for m in LEVELS[1:-1] for s in ("x", "t", "tt") for h in "ab"]
            + ["x64a", "x64b", "tt64a", "tt64b"]
            + ["pq", "gh", "e", "z2", "z3", "z4", "z5", "y", "mean", "var", "gate"])
ACT_STEPS = (["sq", "nrm", "sigw", "siga", "epv", "em", "ep", "gs", "vtok", "atok", "ktok", "mv"]
             + [f"x{m}{h}" for m in LEVELS[1:] for h in "ab"] + ["warm", "pq", "y", "sqc", "std"])
DVE_STEPS = (["kk", "ssm", "inv", "kkn", "ld", "scan", "mid", "mu", "epv", "gs", "tfac", "kp", "rb",
              "at", "b", "bt", "kt", "rt", "bon", "btok"] + [f"gram{i}" for i in range(12)]
             + ["t1"] + [f"{s}{m}{h}" for m in LEVELS[1:-1] for s in ("t", "tt") for h in "ab"] + ["tt64a", "tt64b"]
             + ["gt", "hb", "e", "z2", "z3", "z4", "z5", "yc", "inv2", "y1", "y2", "y3", "y4"])
POOL_STEPS = (["nm1", "tt0", "t0"] + [s for m in LEVELS[1:] for s in (f"nm{m}", f"xz{m}")])


def banks(m, what):
    first = 2 * (LEVELS.index(m) % 2)
    return {"x": 2 - first, "t": first, "tt": 2 - first}[what]


EVEN = {1: (22, 4, (0, 3), (0, 3, 2)), 2: (22, 4, (0, 3), (0, 2)), 4: (11, 8, (0, 6), (0, 4)),
        8: (6, 16, (0, 11), (0, 8)), 16: (3, 32, (0, 22), (0, 16)), 32: (1, 96, (0, 64), (0, 32)),
        64: (1, 96, (0, 64), (0, 64))}
ODD = {2: (22, 4, (1, 4), (2, 4)), 4: (11, 8, (2, 8), (4, 8)), 8: (6, 16, (5, 16), (8, 16)),
       16: (3, 32, (10, 32), (16, 32)), 32: (1, 96, (32, 96), (32, 64)),
       64: (1, 96, (32, 96), (64, 88))}
REST = {2: (22, 4, (2, 4)), 4: (11, 8, (4, 8)), 8: (6, 16, (8, 16)), 16: (3, 32, (16, 32)),
        32: (1, 96, (32, 96)), 64: (1, 96, (64, 96))}


def cut(ap, blocks, stride, part):
    d = ap.ndim
    v = ap[:, 0:blocks * stride] if d == 2 else ap[:, :, 0:blocks * stride]
    part = slice(*part)
    if blocks == 1:
        return v[:, part] if d == 2 else v[:, :, part]
    if d == 2:
        return v.rearrange("p (b s) -> p b s", s=stride)[:, :, part]
    return v.rearrange("p c (b s) -> p c b s", s=stride)[:, :, :, part]


def kept(ap, cols):
    return cut(ap, cols[0], cols[1], cols[3])


def multiplied(ap, cols):
    return cut(ap, cols[0], cols[1], cols[2])


def wide(cols):
    return cols[0] * (cols[2][1] - cols[2][0])


def packed(ap, cols, keep):
    n, lo = cols[2][1] - cols[2][0], cols[2][0]
    part = (cols[3][0] - lo, min(cols[3][1] - lo, n), *cols[3][2:]) if keep else (0, n)
    return cut(ap, cols[0], n, part)


def at(static, per=0, it=0):
    return it * per + static


def step(steps, name, it):
    return at(steps.index(name) + 2, len(steps), it)


def before(steps, it):
    return at(1, len(steps), it)


PACE = dict(ss=2, low=3, vtr=4, bsum=8, atr=4, btr=1, ktr=2, gram0=2, gram1=2, gram2=2, mv=3, x1=2, pq=4, gh=4,
            e=2, z2=3, z3=2, z4=2, z5=2, y=3, mean=3, var=4, gate=4)


def schedule(last):
    rest_ = 96 - sum(PACE.values())
    chain = [n for n in PE_STEPS if n not in PACE and n[-1] == "a"]
    pace, total = [], 0
    for n in PE_STEPS:
        if n in PACE:
            total += PACE[n]
        elif n in chain:
            i = chain.index(n)
            total += (i + 1) * rest_ // len(chain) - i * rest_ // len(chain)
        pace.append(total)
    assert total == 96
    return [min(k, 48) if last else k for k in pace]


Y_FROM = 33


PAR = {}
_n = 0
for _name, _w in (("g_mix", KT), ("g_mlp", KT), ("g_fin", KT), ("mu", 24), ("mu_low", 3), ("mun", 24),
                  ("mun_low", 3), ("conv", 24), ("w0", 8), ("a0", 8), ("k_k", 8), ("k_a", 8),
                  ("nk_a", 8), ("r_k", 8), ("lnw", 8), ("lnb", 8)):
    PAR[_name] = _n
    _n += _w
NPAR = _n
N_PAR = 16 * 16

Q_LOW, T_LOW = 0, 0
Q_RKV0, T_RKV0 = 12, 3
Q_PAIR, T_PAIR = 24, 6
Q_OUT, T_OUT = 24 + 7 * 24 + 12, 6 + 7 * 6 + 3
Q_MLP, T_MLP = Q_OUT + 4 * KT, T_OUT + KT
T_END = T_MLP + FFG * 24
N_CONST = 5 + 12 + 2 + 7 + 2 + 1 + 4


def hybrid_layer(nc, x, meta, norm_mix_g, w_in, shift_mu, conv_w, decay_w0, decay_w2, iclr_a0, iclr_a2,
                 gate_g2, k_k, k_a, r_k, lnx_w, lnx_b, w_out, norm_mlp_g, w_up, w_down, final_norm_g, out):
    ctx = ExitStack()
    sb = lambda name, shape, dt=F32, on=ctx: on.enter_context(nc.sbuf_tensor(name, shape, dt))
    sem = lambda name: ctx.enter_context(nc.semaphore(name))

    res_dram = nc.dram_tensor("residual", [D, T], F32, kind="Internal").ap()
    y_dram = nc.dram_tensor("mixed", [D, T], F32, kind="Internal").ap()
    res_view = res_dram.rearrange("(k p) t -> p k t", p=P)
    y_view = y_dram.rearrange("(k p) t -> p k t", p=P)

    act_hi = sb("act_hi", [P, KT, T], F32R)
    act_lo = sb("act_lo", [P, KT, T], F32R)
    w_raw = sb("w_raw", [P, RAW, KQ, P])
    w_hi = sb("w_hi", [P, RING, KQ, P], F32R)
    w_lo = sb("w_lo", [P, RING, KQ, P], F32R)
    par = sb("par", [P, NPAR])
    ident = sb("ident", [P, P])
    ones = sb("ones", [P, P])
    same_head = sb("same_head", [P, P])
    head_mean = sb("head_mean", [P, P])
    level_mask = sb("level_mask", [P, 7, CP])
    ident_pad = sb("ident_pad", [P, CP])
    zeros = sb("zeros", [P, 66])
    eps_t = sb("eps_t", [P, 2])
    gram_mask = sb("gram_mask", [P, 2, 2, C])

    pre = ExitStack()
    x_rows = sb("x_rows", [P, 4, D], on=pre)
    meta_rows = sb("meta_rows", [META, D], on=pre)
    res0 = sb("res0", [P, KT, T], on=pre)
    sq0 = sb("sq0", [P, 2, T], on=pre)
    rs0 = sb("rs0", [P, T], on=pre)
    nt0 = sb("nt0", [P, 3, T], on=pre)
    blocks = sb("blocks", [P, 6, P], on=pre)
    pre.close()

    mix = ExitStack()
    m_sb = lambda name, shape: sb(name, shape, on=mix)
    shifted = m_sb("shifted", [P, T + 1])
    keep = m_sb("keep", [P, T])
    zr, zk, zv = (m_sb(n, [P, T]) for n in ("zr", "zk", "zv"))
    cx = m_sb("cx", [P, T])
    cu = m_sb("cu", [P, T + 2])
    low_wa = m_sb("low_wa", [P, T])
    low_g = m_sb("low_g", [P, T])
    low_g2 = m_sb("low_g2", [GATE_TAIL, T])
    wa_w = m_sb("wa_w", [P, P])
    g_w = m_sb("g_w", [P, P])
    g_w2 = m_sb("g_w2", [GATE_TAIL, P])
    ones_c = ones[:, 0:C]
    ar = m_sb("ar", [P, NCH, 2, C])
    bt = m_sb("bt", [P, T])
    kt = m_sb("kt", [P, T])
    bonus = m_sb("bonus", [P, T])
    NA = m_sb("NA", [C, 2, NCH, 2, CP])
    KA = m_sb("KA", [C, 2, NCH, 2, CP])
    AMV = m_sb("AMV", [C, 2, NCH, P])
    v_tok = m_sb("v_tok", [C, NCH, P])
    b_tok = m_sb("b_tok", [C, NCH, P])
    k_tok = m_sb("k_tok", [C, NCH, P])
    GT = m_sb("GT", [P, 4, P])
    HB = m_sb("HB", [P, 5, P])
    ZB = m_sb("ZB", [P, 4, P])
    mid = m_sb("mid", [P, NCH])
    gs = m_sb("gs", [P, 5])
    warm = m_sb("warm", [P, 1])
    uni = m_sb("uni", [P, 9 * T])
    ld, mu, ep, em, epv, asig, kk, kp, fsq = (uni[:, i * T:(i + 1) * T] for i in range(9))
    W = NCH * CP
    TM, XM, TTM, NM = (uni[0:C, 2 * i * W:2 * (i + 1) * W].rearrange("p (h c n) -> p h c n", h=2, c=NCH)
                       for i in range(4))
    PQ = uni[0:C, 0:12 * P].rearrange("p (h c n) -> p h c n", h=2, c=NCH)
    ybuf, ycen = uni[:, 4 * W:4 * W + T], uni[:, 4 * W + T:4 * W + 2 * T]
    ET = uni[:, 6 * W:6 * W + 5 * C].rearrange("p (c n) -> p c n", c=5)
    ysq = uni[:, 0:T]
    mix.close()

    post = ExitStack()
    u_hi = sb("u_hi", [P, UT, T], F32R, on=post)
    u_lo = sb("u_lo", [P, UT, T], F32R, on=post)
    res = sb("res", [P, KT, T], on=post)
    sq1 = sb("sq1", [P, 2, T], on=post)
    rs1 = sb("rs1", [P, T], on=post)
    nt1 = sb("nt1", [P, 3, T], on=post)
    rows = sb("rows", [P, D], on=post)
    post.close()
    yin = ctx.enter_context(nc.sbuf_tensor("yin", [P, 2, T], F32))

    PD = ctx.enter_context(nc.psum_tensor("PD", [P, 4, 512], F32))
    PW = ctx.enter_context(nc.psum_tensor("PW", [P, 4, 512], F32))

    x_loaded = [sem(f"x_loaded{i}") for i in range(5)]
    par_loaded = sem("par_loaded")
    consts_made = sem("consts_made")
    par_derived = sem("par_derived")
    x_turned = sem("x_turned")
    x_kept = [sem("x_kept_dve"), sem("x_kept_act")]
    raw_loaded = [sem(f"raw_loaded{i}") for i in range(RAW)]
    raw_zeroed = sem("raw_zeroed")
    hi_split = sem("hi_split")
    lo_split = sem("lo_split")
    quarter_used = sem("quarter_used")
    evacuated = [sem("evacuated0"), sem("evacuated1")]
    squared = sem("squared")
    summed = sem("summed")
    rooted = sem("rooted")
    rs_ready = sem("rs_ready")
    normed = sem("normed")
    act_hi_ready = sem("act_hi_ready")
    act_ready = sem("act_ready")
    res_loaded = sem("res_loaded")
    pe_done, act_done, dve_done, pool_done = (sem(f"pair_steps_{e}") for e in ("pe", "act", "dve", "pool"))
    wa_loaded, g_loaded = sem("wa_loaded"), sem("g_loaded")
    low_done = sem("low_done")
    z_done = sem("z_done")
    conv_step = sem("conv_step")
    conv_stored, y_stored = sem("conv_stored"), sem("y_stored")
    zeroed = sem("zeroed")
    y_loaded = [sem("y_loaded0"), sem("y_loaded1")]
    y_hi, y_ready = sem("y_hi"), sem("y_ready")
    u_sq, u_hi_ready, u_ready = sem("u_sq"), sem("u_hi_ready"), sem("u_ready")
    fin_turned, fin_kept, rows_stored = sem("fin_turned"), [sem("fin_kept_dve"), sem("fin_kept_act")], sem("rows_stored")

    def p_(name, i, n=1):
        return par[:, PAR[name] + i:PAR[name] + i + n]

    def halves(ap):
        return ap.rearrange("p (a n) -> p a n", a=2)

    def pd(n):
        return PD[:, 2 * (n % 2):2 * (n % 2) + 2, 0:HALF]

    def pw(b):
        return PW[:, b:b + 2, 0:HALF]

    def xbank(b):
        return (PD if b % 8 < 4 else PW)[:, b % 4, :]

    def free(n):
        return n // 2 + 1

    win_q = w_in.rearrange("(a k p) n -> a p k n", k=KQ, p=P)
    conv_q = win_q[:, :, :, 0:CONV].rearrange("a p k (s m n) -> a p k s m n", s=3, n=P)
    rkv_q = win_q[:, :, :, CONV:LOWR].rearrange("a p k (s m n) -> a p k s m n", s=3, n=P)
    wout_q = w_out.rearrange("(a k p) (m n) -> a p k m n", k=KQ, p=P, n=P)
    wup_q = w_up.rearrange("(a k p) (g m n) -> a p k g m n", k=KQ, p=P, g=FFG, n=P)
    wdn_q = w_down.rearrange("(g a k p) (m n) -> g a p k m n", g=FFG, k=KQ, p=P, n=P)

    NORM = [(res0, sq0, rs0, nt0, "g_mix"), (res, sq1, rs1, nt1, "g_mlp"), (res, sq1, rs1, nt1, "g_fin")]

    block = ctx.enter_context(nc.Block())

    @block.sync
    def _(sp):
        sp.dma_start(meta_rows[:], meta).then_inc(x_loaded[0], 16)
        for i in range(4):
            sp.dma_start(x_rows[:, i, :], x[i * P:(i + 1) * P, :]).then_inc(x_loaded[i + 1], 16)

        def load(src, q, per=0, it=0, width=P):
            if q >= RAW:
                sp.wait_ge(lo_split, at(q - RAW + 1, per, it))
            sp.dma_start(w_raw[:, q % RAW, :, 0:width], src).then_inc(raw_loaded[q % RAW], 16)

        q = Q_LOW
        sp.wait_ge(raw_zeroed, 1)
        for first, width in ((LOWR + 2 * P, GATE_TAIL), (LOWR, P), (LOWR + P, P)):
            for a in range(4):
                load(win_q[a, :, :, first:first + width], q, width=width)
                q += 1
        for s in range(3):
            for a in range(4):
                load(rkv_q[a, :, :, s, 0, :], q)
                q += 1
        with sp.Fori(0, PAIRS - 1) as j:
            q = Q_PAIR
            for s in (0, 2, 1):
                for a in range(4):
                    load(conv_q[a, :, :, s, j, :], q, 24, j)
                    q += 1
            for s in range(3):
                for a in range(4):
                    load(rkv_q[a, :, :, s, j + 1, :], q, 24, j)
                    q += 1
        q = Q_PAIR + 7 * 24
        for s in (0, 2, 1):
            for a in range(4):
                load(conv_q[a, :, :, s, PAIRS - 1, :], q)
                q += 1
        def load_out(i):
            for n in range(2):
                for a in range(4):
                    load(wout_q[a, :, :, i * 2 + n, :], Q_OUT + 4 * n + a, 8, i)

        load_out(0)
        for k in range(KT - 1):
            if k < PAIRS:
                sp.wait_ge(conv_stored, 16 * (k + 2))
            else:
                sp.wait_ge(y_stored, 16 * (k - PAIRS + 2))
            if k >= 2:
                sp.wait_ge(y_ready, k - 1)
            sp.dma_start(yin[:, k % 2, :], y_view[:, k, :]).then_inc(y_loaded[k % 2], 16)
        with sp.Fori(1, KT // 2) as i:
            load_out(i)
        with sp.Fori(0, FFG) as g:
            for m in range(UT):
                for a in range(4):
                    load(wup_q[a, :, :, g, m, :], Q_MLP + 4 * m + a, 64, g)
            for m in range(KT):
                for a in range(2):
                    load(wdn_q[g, a, :, :, m, :], Q_MLP + 32 + 2 * m + a, 64, g)

    @block.gpsimd
    def _(pool):
        made = [0]

        def const(ins, wait=True):
            made[0] += 1
            ins.then_inc(consts_made, 1)
            if wait:
                pool.wait_ge(consts_made, made[0])

        nc.gpsimd.memset(w_raw[:], 0.0).then_inc(raw_zeroed, 1)
        const(nc.gpsimd.memset(ident[:], 0.0))
        const(nc.gpsimd.affine_select(out=ident[:], in_=ident[:], compare_op=ALU.not_equal, fill=1.0, base=0,
                                      pattern=[[-1, P]], channel_multiplier=1))
        const(nc.gpsimd.memset(ones[:], 1.0))
        const(nc.gpsimd.memset(zeros[:], 0.0))
        const(nc.gpsimd.memset(blocks[:], 1.0))
        for i, m in enumerate(LEVELS[1:]):
            v = blocks[:, i, :].rearrange("p (b n) -> p b n", n=m)
            const(nc.gpsimd.affine_select(out=v, in_=v, compare_op=ALU.is_ge, fill=0.0, base=0,
                                          pattern=[[-m, P // m], [0, m]], channel_multiplier=1))
            const(nc.gpsimd.affine_select(out=v, in_=v, compare_op=ALU.is_ge, fill=0.0, base=m - 1,
                                          pattern=[[m, P // m], [0, m]], channel_multiplier=-1))
        const(nc.gpsimd.tensor_copy(ident_pad[:], ident[:, 0:CP]))
        const(nc.gpsimd.memset(ident_pad[:, C:CP], 0.0))
        const(nc.gpsimd.tensor_tensor(level_mask[:, 0, :], blocks[:, 0, 0:CP], ident[:, 0:CP], ALU.subtract))
        for i in range(1, 6):
            const(nc.gpsimd.tensor_tensor(level_mask[:, i, :], blocks[:, i, 0:CP], blocks[:, i - 1, 0:CP], ALU.subtract))
        const(nc.gpsimd.tensor_tensor(level_mask[:, 6, :], ones[:, 0:CP], blocks[:, 5, 0:CP], ALU.subtract))
        const(nc.gpsimd.tensor_copy(same_head[:], blocks[:, 5, :]))
        const(nc.gpsimd.tensor_scalar(head_mean[:], blocks[:, 5, :], 1.0 / HS, None, ALU.mult))
        const(nc.gpsimd.memset(gram_mask[:], 1.0))
        for c in range(2):
            for strict in range(2):
                v = gram_mask[:, c, 1 - strict, :]
                const(nc.gpsimd.affine_select(out=v, in_=v, compare_op=ALU.is_ge, fill=0.0, base=-strict,
                                              pattern=[[1, C]], channel_multiplier=-1))

        pool.wait_ge(x_kept[0], 9)
        pool.wait_ge(x_kept[1], 8)
        pool.dma_start(res_view[:, 0:KT // 2, :], res0[:, 0:KT // 2, :]).then_inc(conv_stored, 16)
        pool.dma_start(res_view[:, KT // 2:KT, :], res0[:, KT // 2:KT, :]).then_inc(y_stored, 16)

        pool.wait_ge(act_ready, KT)
        pool.wait_ge(conv_stored, 16)
        pool.wait_ge(y_stored, 16)
        nc.gpsimd.memset(NA[:], 0.0)
        nc.gpsimd.memset(shifted[:, 0:1], 0.0)
        nc.gpsimd.memset(cu[:, 0:2], 0.0)
        nc.gpsimd.memset(GT[:], 0.0)
        nc.gpsimd.memset(HB[:], 0.0).then_inc(zeroed, 1)
        pool.wait_ge(zeroed, 1)
        pool.sem_inc(pool_done, 1)

        def load_wa(j):
            pool.dma_start(wa_w[0:HS, :], decay_w2[:, bass.ts(j, P)]).then_inc(wa_loaded, 16)
            pool.dma_start(wa_w[HS:P, :], iclr_a2[:, bass.ts(j, P)]).then_inc(wa_loaded, 16)

        def load_g(j):
            pool.dma_start(g_w[:], gate_g2[0:P, bass.ts(j, P)]).then_inc(g_loaded, 16)
            pool.dma_start(g_w2[:], gate_g2[P:P + GATE_TAIL, bass.ts(j, P)]).then_inc(g_loaded, 16)

        def pair(j, last=False):
            n = [0]

            def done(name, ins):
                assert POOL_STEPS[n[0]] == name
                n[0] += 1
                ins.then_inc(pool_done, 1)

            if not last:
                pool.wait_ge(pe_done, step(PE_STEPS, "low", j))
                load_wa(j + 1)

            def mask_n(i):
                m = LEVELS[i]
                nc_ = level_mask[0:C, i, :].unsqueeze(1).to_broadcast([C, NCH, CP])
                for h in range(2):
                    ins = nc.gpsimd.tensor_tensor(NM[:, h, :, :], NA[:, h, :, 0, :], nc_, ALU.mult)
                done(f"nm{m}", ins)

            idp = ident_pad[0:C, :].unsqueeze(1).to_broadcast([C, NCH, CP])
            pool.wait_ge(dve_done, step(DVE_STEPS, "gram5", j))
            pool.wait_ge(dve_done, step(DVE_STEPS, "btok", j))
            mask_n(0)
            pool.wait_ge(pool_done, step(POOL_STEPS, "nm1", j))
            for h in range(2):
                ins = nc.gpsimd.tensor_tensor(TTM[:, h, :, :], NM[:, h, :, :], idp, ALU.add)
            done("tt0", ins)
            for h in range(2):
                ins = nc.gpsimd.tensor_copy(TM[:, h, :, :], idp)
            done("t0", ins)
            for i, m in enumerate(LEVELS[1:], 1):
                pool.wait_ge(pe_done, step(PE_STEPS, "x1" if m == 2 else f"x{m // 2}b", j))
                if m == 2:
                    pool.wait_ge(pool_done, step(POOL_STEPS, "t0", j))
                mask_n(i)
                if m > 2:
                    pool.wait_ge(pe_done, step(PE_STEPS, f"tt{m // 2}b", j))
                blocks_, _, part = REST[m]
                w = part[1] - part[0]
                nil = cut(zeros[0:C, 0:blocks_ * w].unsqueeze(1).to_broadcast([C, NCH, blocks_ * w]), blocks_, w, (0, w))
                for h in range(2):
                    ins = nc.gpsimd.tensor_tensor(cut(XM[:, h, :, :], *REST[m]), nil, nil, ALU.mult)
                done(f"xz{m}", ins)
                if m == 32:
                    store_conv(j)
            if not last:
                pool.wait_ge(dve_done, step(DVE_STEPS, "y4", j))
                pool.dma_start(y_view[:, bass.ds(j + PAIRS, 1), :], bt[:].unsqueeze(1)).then_inc(y_stored, 16)
                load_g(j + 1)

        def store_conv(j):
            pool.wait_ge(evacuated[0], at(free(T_PAIR + 2), 3, j))
            pool.dma_start(y_view[:, bass.ds(j, 1), :], cx[:].unsqueeze(1)).then_inc(conv_stored, 16)

        load_wa(0)
        load_g(0)
        with pool.Fori(0, PAIRS - 1) as j:
            pair(j)
        pair(PAIRS - 1, last=True)
        pool.wait_ge(y_ready, KT)
        pool.dma_start(res[:], res_view).then_inc(res_loaded, 16)
        for t in range(4):
            pool.wait_ge(fin_kept[0], 2 * (t + 1))
            pool.wait_ge(fin_kept[1], 2 * (t + 1))
            pool.dma_start(out[t * P:(t + 1) * P, :], rows[:]).then_inc(rows_stored, 16)
        pool.wait_ge(rows_stored, 64)
        pool.wait_ge(conv_stored, 16 * (PAIRS + 1))
        pool.wait_ge(y_stored, 16 * PAIRS)

    @block.scalar
    def _(act):
        fm = lambda p: p.rearrange("(t p) -> p t", p=P)
        n_par = 0
        for name, src in (("g_mix", fm(norm_mix_g)), ("g_mlp", fm(norm_mlp_g)), ("g_fin", fm(final_norm_g)),
                          ("mu", fm(shift_mu[0:3 * DH])), ("mu_low", fm(shift_mu[3 * DH:3 * DH + 2 * P])),
                          ("w0", fm(decay_w0)), ("a0", fm(iclr_a0)), ("k_k", fm(k_k)), ("k_a", fm(k_a)),
                          ("r_k", fm(r_k)),
                          ("lnw", fm(lnx_w)), ("lnb", fm(lnx_b))):
            act.dma_start(par[:, PAR[name]:PAR[name] + src.shape[1]], src, allow_slow_non_contiguous=True).then_inc(par_loaded, 16)
            n_par += 16
        for w in range(3):
            act.dma_start(p_("conv", 8 * w, 8), fm(conv_w[w]), allow_slow_non_contiguous=True).then_inc(par_loaded, 16)
            n_par += 16
        act.dma_start(par[0:GATE_TAIL, PAR["mu_low"] + 2:PAR["mu_low"] + 3],
                      shift_mu[3 * DH + 2 * P:3 * DH + 2 * P + GATE_TAIL].rearrange("(p t) -> p t", t=1),
                      allow_slow_non_contiguous=True).then_inc(par_loaded, 16)
        n_par += 16
        assert n_par == N_PAR

        for b in range(1, 17, 2):
            act.wait_ge(x_turned, b + 1)
            t, k4 = divmod(b - 1, 4)
            nc.scalar.copy(res0[:, 4 * k4:4 * k4 + 4, META + P * t:META + P * (t + 1)],
                           xbank(b).rearrange("p (k n) -> p k n", k=4)).then_inc(x_kept[1], 1)
        act.wait_ge(x_kept[0], 9)
        act.wait_ge(x_kept[1], 8)

        def norm(i):
            res_, sq, rs, nt, _ = NORM[i]
            for k in range(KT):
                if k >= 2:
                    act.wait_ge(summed, KT * i + k - 1)
                nc.scalar.activation(sq[:, k % 2, :], res_[:, k, :], ACT.Square).then_inc(squared, 1)
            act.wait_ge(summed, KT * (i + 1))
            nc.scalar.activation(halves(rs[:]), pw(0), ACT.Sqrt, bias=eps_t[:, 0:1], scale=1.0 / D).then_inc(rooted, 1)
            if i < 2:
                for k in range(KT):
                    act.wait_ge(normed, KT * i + k + 1)
                    nc.scalar.copy(act_hi[:, k, :], nt[:, k % 3, :]).then_inc(act_hi_ready, 1)

        act.wait_ge(par_derived, 4)
        norm(0)

        def split(q, per=0, it=0):
            act.wait_ge(raw_loaded[q % RAW], at(16 * (q // RAW + 1), 16 * per // RAW, it))
            if q >= RING:
                act.wait_ge(quarter_used, at(q - RING + 1, per, it))
            nc.scalar.copy(w_hi[:, q % RING], w_raw[:, q % RAW]).then_inc(hi_split, 1)

        def take_shifted(n, q_done, mun, per_q=0, it=0, z_before=None, rows_=P):
            act.wait_ge(quarter_used, at(q_done, per_q, it))
            if z_before is not None:
                act.wait_ge(z_done, z_before)
            nc.scalar.copy(halves(shifted[0:rows_, 1:T + 1]), pd(n)[0:rows_])
            nc.scalar.activation(halves(keep[0:rows_, :]), pd(n)[0:rows_], ACT.Copy, scale=mun).then_inc(evacuated[n % 2], 1)

        for q in range(Q_LOW, Q_LOW + 2 * LEAD):
            split(q)
        act.wait_ge(zeroed, 1)
        for n in range(6):
            mun = p_("mun_low", (2, 0, 1)[n]) if n < 3 else p_("mun", 8 * (n - 3))
            rows_ = P if n else GATE_TAIL
            take_shifted(n, 4 * (n + 1), mun[0:rows_], z_before=n if n else None, rows_=rows_)
            for q in range(4 * n + 8, 4 * n + 12):
                if q < Q_PAIR + LEAD:
                    split(q)
            if n == 0:
                act.wait_ge(z_done, 1)
                nc.scalar.activation(low_g2[:], low_g2[:], ACT.Sigmoid).then_inc(low_done, 1)
            if n == 1:
                act.wait_ge(z_done, 2)
                nc.scalar.activation(low_wa[0:HS, :], low_wa[0:HS, :], ACT.Tanh).then_inc(low_done, 1)
            if n == 2:
                act.wait_ge(z_done, 3)
                nc.scalar.activation(low_g[:], low_g[:], ACT.Sigmoid).then_inc(low_done, 1)

        def split_y(k):
            if k == 0:
                act.wait_ge(quarter_used, Q_OUT)
            if k < KT - 1:
                act.wait_ge(y_loaded[k % 2], 16 * (k // 2 + 1))
            else:
                act.wait_ge(dve_done, step(DVE_STEPS, "y4", PAIRS - 1))
            nc.scalar.copy(act_hi[:, k, :], yin[:, k % 2, :] if k < KT - 1 else bt[:]).then_inc(y_hi, 1)

        def pair(j, last=False):
            n_done = [0]

            def done(name, ins):
                assert ACT_STEPS[n_done[0]] == name, (name, ACT_STEPS[n_done[0]])
                n_done[0] += 1
                ins.then_inc(act_done, 1)
                own(name)

            pe = lambda name: act.wait_ge(pe_done, step(PE_STEPS, name, j))
            dve = lambda name: act.wait_ge(dve_done, step(DVE_STEPS, name, j))
            own = lambda name: act.wait_ge(act_done, step(ACT_STEPS, name, j))
            feat = lambda name, w=1: par[:, bass.ds(j + PAR[name], 1)]

            def steps_of(name):
                if name == "ss":
                    done("sq", nc.scalar.activation(fsq, zk[:], ACT.Square, scale=feat("k_k")))
                    dve("ssm")
                    done("nrm", nc.scalar.activation(fsq, fsq, ACT.Sqrt))
                if name == "low":
                    pe("low")
                    done("sigw", nc.scalar.activation(halves(ld), pw(0), ACT.Sigmoid, bias=feat("w0")))
                    done("siga", nc.scalar.activation(halves(asig), pw(2), ACT.Sigmoid, bias=feat("a0")))
                if name == "vtr":
                    dve("epv")
                    done("epv", nc.scalar.activation(epv, epv, ACT.Exp))
                    done("em", nc.scalar.activation(em, mu, ACT.Exp, scale=-1.0))
                    done("ep", nc.scalar.activation(ep, mu, ACT.Exp))
                    dve("gs")
                    done("gs", nc.scalar.activation(gs[:], gs[:], ACT.Exp))
                    pe("vtr")
                    done("vtok", nc.scalar.copy(v_tok[:].rearrange("p (a c) n -> p a (c n)", a=2), PW[0:C, 0:2, 0:384]))
                if name == "atr":
                    pe("atr")
                    for a in range(2):
                        ins = nc.scalar.copy(AMV[:, :, 3 * a:3 * a + 3, 0:HS].rearrange("p h c n -> p c h n"),
                                             PW[0:C, 2 + a, 0:384].rearrange("p (c h n) -> p c h n", c=3, h=2))
                    done("atok", ins)
                if name == "ktr":
                    pe("ktr")
                    done("ktok", nc.scalar.copy(k_tok[:].rearrange("p (a c) n -> p a (c n)", a=2), PW[0:C, 2:4, 0:384]))
                if name == "mv":
                    pe("mv")
                    for h in range(2):
                        ins = nc.scalar.copy(AMV[:, h, :, HS:P], PW[0:C, h, 0:384].rearrange("p (c n) -> p c n", c=NCH))
                    done("mv", ins)
                if name[0] == "x" and name != "x1":
                    m, h = int(name[1:-1]), "ab".index(name[-1])
                    pe(name)
                    w = wide(EVEN[m])
                    done(name, nc.scalar.copy(
                        kept(XM[:, h, :, :], EVEN[m]),
                        packed(PW[0:C, banks(m, "x") + h, 0:NCH * w].rearrange("p (c n) -> p c n", c=NCH), EVEN[m], True)))
                if name == "tt64b":
                    done("warm", nc.scalar.activation(warm[:], eps_t[:, 0:1], ACT.Sqrt))
                if name == "pq":
                    pe("pq")
                    done("pq", nc.scalar.copy(PQ.rearrange("p h c n -> p (h c n)"),
                                              PW[0:C, 0:3, :].rearrange("p a n -> p (a n)")))
                if name == "y":
                    pe("y")
                    done("y", nc.scalar.copy(halves(ybuf), pw(2)))
                if name == "mean":
                    dve("yc")
                    done("sqc", nc.scalar.activation(ysq, ycen, ACT.Square))
                if name == "var":
                    pe("var")
                    done("std", nc.scalar.activation(halves(ysq), pw(2), ACT.Sqrt, bias=eps_t[:, 1:2]))

            splits, tiles, y_split = 0, 0, 0
            for i, (name, k) in enumerate(zip(PE_STEPS, schedule(last))):
                steps_of(name)
                while splits < k // KQ:
                    split(Q_PAIR + LEAD + splits, 24, j)
                    splits += 1
                while 16 * (tiles + 1) <= k:
                    n = T_PAIR + tiles
                    if tiles == 0:
                        act.wait_ge(quarter_used, at(Q_PAIR + 4, 24, j))
                        act.wait_ge(conv_stored, at(16, 16, j))
                        nc.scalar.copy(halves(cx[:]), pd(n)).then_inc(evacuated[n % 2], 1)
                    if tiles >= 3:
                        take_shifted(n, Q_PAIR + 4 * (tiles + 1), par[:, bass.ds(j + (PAR["mun"] + 8 * (tiles - 3) + 1), 1)],
                                     24, j, z_before=at(6 + tiles - 3, 3, j))
                    tiles += 1
                if last and i >= Y_FROM and y_split < KT - 1:
                    split_y(y_split)
                    y_split += 1
            assert n_done[0] == len(ACT_STEPS) and (not last or y_split == KT - 1)

        act.sem_inc(act_done, 1)
        with act.Fori(0, PAIRS - 1) as j:
            pair(j)
        pair(PAIRS - 1, last=True)

        split_y(KT - 1)

        with act.Fori(0, KT // 2) as i:
            for q in range(8):
                split(Q_OUT + LEAD + q, 8, i)
        for n in range(T_OUT, T_MLP):
            act.wait_ge(evacuated[n % 2], free(n))
        norm(1)

        def mlp_group(g, last=False):
            for m in range(UT):
                for a in range(4):
                    split(Q_MLP + LEAD + 4 * m + a, 64, g)
                n = T_MLP + m
                act.wait_ge(quarter_used, at(Q_MLP + 4 * (m + 1), 64, g))
                if m >= 3:
                    act.wait_ge(u_ready, at(m - 2, UT, g))
                nc.scalar.activation(halves(nt1[:, m % 3, :]), pd(n), ACT.Relu).then_inc(evacuated[n % 2], 1)
                act.wait_ge(u_sq, at(m + 1, UT, g))
                nc.scalar.copy(u_hi[:, m, :], nt1[:, m % 3, :]).then_inc(u_hi_ready, 1)
            for q in range(4 * UT, 64 - (LEAD if last else 0)):
                split(Q_MLP + LEAD + q, 64, g)

        with act.Fori(0, FFG - 1) as g:
            mlp_group(g)
        mlp_group(FFG - 1, last=True)
        for n in range(T_END - KT, T_END):
            act.wait_ge(evacuated[n % 2], free(n))
        norm(2)
        for b in range(1, 16, 2):
            act.wait_ge(fin_turned, b + 1)
            if b > 3:
                act.wait_ge(rows_stored, 16 * (b // 4))
            nc.scalar.copy(rows[:, (b % 4) * 512:(b % 4 + 1) * 512], xbank(b)).then_inc(fin_kept[1], 1)

    @block.vector
    def _(dve):
        V = nc.vector
        V.memset(eps_t[:, 0:1], NORM_EPS)
        V.memset(eps_t[:, 1:2], LNX_EPS)
        dve.wait_ge(par_loaded, N_PAR)
        one_minus = lambda o, i: V.tensor_scalar(o, i, -1.0, 1.0, ALU.mult, ALU.add)
        one_minus(p_("mun", 0, 24), p_("mu", 0, 24)).then_inc(par_derived, 1)
        one_minus(p_("mun_low", 0, 2), p_("mu_low", 0, 2)).then_inc(par_derived, 1)
        one_minus(p_("mun_low", 2)[0:GATE_TAIL], p_("mu_low", 2)[0:GATE_TAIL]).then_inc(par_derived, 1)
        one_minus(p_("nk_a", 0, 8), p_("k_a", 0, 8)).then_inc(par_derived, 1)
        dve.wait_ge(par_derived, 4)

        for b in range(0, 17, 2):
            dve.wait_ge(x_turned, b + 1)
            if b == 0:
                dst, src = res0[:, :, 0:META], xbank(0)[:, 0:KT * META].rearrange("p (k n) -> p k n", k=KT)
            else:
                t, k4 = divmod(b - 1, 4)
                dst = res0[:, 4 * k4:4 * k4 + 4, META + P * t:META + P * (t + 1)]
                src = xbank(b).rearrange("p (k n) -> p k n", k=4)
            V.tensor_copy(dst, src).then_inc(x_kept[0], 1)

        def norm(i):
            res_, _, rs, nt, gain = NORM[i]
            dve.wait_ge(rooted, i + 1)
            V.reciprocal(rs[:], rs[:]).then_inc(rs_ready, 1)
            dve.wait_ge(rs_ready, i + 1)

            def low(k):
                dve.wait_ge(act_hi_ready, KT * i + k + 1)
                V.tensor_tensor(act_lo[:, k, :], nt[:, k % 3, :], act_hi[:, k, :].bitcast(F32),
                                ALU.subtract).then_inc(act_ready, 1)

            for k in range(KT):
                if i < 2 and k >= 3:
                    dve.wait_ge(act_ready, KT * i + k - 2)
                V.scalar_tensor_tensor(nt[:, k % 3, :] if i < 2 else res_[:, k, :], res_[:, k, :], p_(gain, k),
                                       rs[:], ALU.mult, ALU.mult).then_inc(normed, 1)
                if i < 2 and k:
                    low(k - 1)
            if i < 2:
                low(KT - 1)

        norm(0)

        def split(q, per=0, it=0):
            dve.wait_ge(hi_split, at(q + 1, per, it))
            V.tensor_tensor(w_lo[:, q % RING], w_raw[:, q % RAW], w_hi[:, q % RING].bitcast(F32),
                            ALU.subtract).then_inc(lo_split, 1)

        def shift(n, dst, mu_, per=0, it=0, rows_=P):
            dve.wait_ge(evacuated[n % 2], at(free(n), per, it))
            V.scalar_tensor_tensor(dst, shifted[0:rows_, 0:T], mu_, keep[0:rows_, :], ALU.mult,
                                   ALU.add).then_inc(z_done, 1)

        for q in range(Q_LOW, Q_LOW + 2 * LEAD):
            split(q)
        dve.wait_ge(zeroed, 1)
        for n, dst in enumerate((low_g2, low_wa, low_g, zr, zk, zv)):
            m_ = p_("mu_low", (2, 0, 1)[n]) if n < 3 else p_("mu", 8 * (n - 3))
            rows_ = P if n else GATE_TAIL
            shift(n, dst[:], m_[0:rows_], rows_=rows_)
            for q in range(4 * n + 8, 4 * n + 12):
                if q < Q_PAIR + LEAD:
                    split(q)

        def split_y(k):
            dve.wait_ge(y_hi, k + 1)
            V.tensor_tensor(act_lo[:, k, :], yin[:, k % 2, :] if k < KT - 1 else bt[:],
                            act_hi[:, k, :].bitcast(F32), ALU.subtract).then_inc(y_ready, 1)

        def pair(j, last=False):
            n_done = [0]

            def done(name, ins):
                assert DVE_STEPS[n_done[0]] == name, (name, DVE_STEPS[n_done[0]])
                n_done[0] += 1
                ins.then_inc(dve_done, 1)
                own(name)

            pe = lambda name: dve.wait_ge(pe_done, step(PE_STEPS, name, j))
            act = lambda name: dve.wait_ge(act_done, step(ACT_STEPS, name, j))
            pool = lambda name: dve.wait_ge(pool_done, step(POOL_STEPS, name, j))
            own = lambda name: dve.wait_ge(dve_done, step(DVE_STEPS, name, j))
            feat = lambda name: par[:, bass.ds(j + PAR[name], 1)]
            chunks = lambda ap: ap.rearrange("p (c n) -> p c n", c=NCH)

            def steps_of(name):
                if name == "ss":
                    done("kk", V.tensor_scalar(kk, zk[:], feat("k_k"), None, ALU.mult))
                    pe("ss")
                    done("ssm", V.tensor_scalar(halves(fsq), pw(2), 1e-24, None, ALU.max))
                    act("nrm")
                    done("inv", V.reciprocal(fsq, fsq))
                    done("kkn", V.tensor_tensor(kk, kk, fsq, ALU.mult))
                if name == "low":
                    act("sigw")
                    done("ld", V.tensor_scalar(ld, ld, -math.exp(-0.5), None, ALU.mult))
                    for c in range(NCH):
                        ins = V.tensor_tensor_scan(mu[:, c * C:(c + 1) * C], ones_c, ld[:, c * C:(c + 1) * C],
                                                   0.0, ALU.mult, ALU.add)
                    done("scan", ins)
                    done("mid", V.tensor_copy(mid[:].unsqueeze(2), chunks(mu)[:, :, MID:MID + 1]))
                    done("mu", V.tensor_tensor(chunks(mu), chunks(mu), mid[:].unsqueeze(2).to_broadcast([P, NCH, C]),
                                               ALU.subtract))
                    done("epv", V.tensor_tensor(epv, mu, ld, ALU.subtract))
                    done("gs", V.tensor_tensor(gs[:].unsqueeze(2), chunks(mu)[:, 0:NCH - 1, C - 1:C],
                                               mid[:, 1:NCH].unsqueeze(2), ALU.add))
                    act("siga")
                    done("tfac", V.tensor_scalar(kp, asig, feat("k_a"), feat("nk_a"), ALU.mult, ALU.add))
                    done("kp", V.tensor_tensor(kp, zk[:], kp, ALU.mult))
                    done("rb", V.scalar_tensor_tensor(ld, zr[:], feat("r_k"), kp, ALU.mult, ALU.mult))
                if name == "vtr":
                    act("epv")
                    done("at", V.scalar_tensor_tensor(ar[:, :, 0, :], chunks(kk), -1.0, chunks(epv), ALU.mult, ALU.mult))
                    done("b", V.tensor_tensor(asig, kk, asig, ALU.mult))
                    act("em")
                    dve.wait_ge(y_stored, at(16, 16, j))
                    done("bt", V.tensor_tensor(bt[:], asig, em, ALU.mult))
                    done("kt", V.tensor_tensor(kt[:], kp, em, ALU.mult))
                    act("ep")
                    done("rt", V.tensor_tensor(ar[:, :, 1, :], chunks(zr[:]), chunks(ep), ALU.mult))
                if name == "bsum":
                    pe("bsum")
                    done("bon", V.tensor_tensor(halves(bonus[:]), pw(2), halves(zv[:]), ALU.mult))
                if name == "btr":
                    pe("btr")
                    done("btok", V.tensor_copy(b_tok[:].rearrange("p (a c) n -> p a (c n)", a=2), PW[0:C, 0:2, 0:384]))
                if name in ("gram0", "gram1", "gram2"):
                    pe(name)
                    for i in range(4 * int(name[4]), 4 * int(name[4]) + 4):
                        h, c2 = divmod(i % 6, 3)
                        done(f"gram{i}", V.tensor_tensor(
                            (NA if i < 6 else KA)[:, h, 2 * c2:2 * c2 + 2, :, 0:C],
                            PW[0:C, i % 4, 0:4 * C].rearrange("p (c s n) -> p c s n", c=2, s=2),
                            gram_mask[0:C], ALU.mult))

                def update(mat, which, bank, h):
                    n = wide(which)
                    dst = kept(mat[:, h, :, :], which)
                    src = packed(PW[0:C, bank + h, 0:NCH * n].rearrange("p (c n) -> p c n", c=NCH), which, True)
                    return V.tensor_tensor(dst, src, dst, ALU.add)

                if name == "x1":
                    pe("x1")
                    pool("t0")
                    update(TM, EVEN[1], 2, 0)
                    done("t1", update(TM, EVEN[1], 2, 1))
                if name[0] == "t" and name[-1] in "ab":
                    what = name[:2] if name[1] == "t" else "t"
                    m, h = int(name[len(what):-1]), "ab".index(name[-1])
                    pe(name)
                    if what == "t":
                        done(name, update(TM, EVEN[m], banks(m, "t"), h))
                    else:
                        done(name, update(TTM, ODD[m], banks(m, "tt"), h))
                if name == "gh":
                    pe("gh")
                    for h in range(2):
                        hs = slice(HS * h, HS * (h + 1))
                        ins = V.tensor_tensor(GT[hs, :, hs], PW[hs, 0, 0:4 * HS].rearrange("p (c n) -> p c n", c=4),
                                              ident[hs, hs].unsqueeze(1).to_broadcast([HS, 4, HS]), ALU.add)
                    done("gt", ins)
                    for h in range(2):
                        hs = slice(HS * h, HS * (h + 1))
                        ins = V.tensor_tensor(HB[hs, :, hs], PW[hs, 1, 0:5 * HS].rearrange("p (c n) -> p c n", c=5),
                                              gs[hs].unsqueeze(2).to_broadcast([HS, 5, HS]), ALU.mult)
                    done("hb", ins)
                if name == "e":
                    pe("e")
                    done("e", V.tensor_tensor(ET, PW[:, 2, 0:5 * C].rearrange("p (c n) -> p c n", c=5),
                                              ar[:, 1:NCH, 1, :], ALU.add))
                if name in ("z2", "z3", "z4", "z5"):
                    c = int(name[1]) - 1
                    pe(name)
                    done(name, V.scalar_tensor_tensor(ZB[:, c - 1, :], PW[:, (c - 1) % 2, 0:P], gs[:, c:c + 1],
                                                      HB[:, c, :], ALU.mult, ALU.add))
                if name == "mean":
                    pe("mean")
                    done("yc", V.tensor_tensor(halves(ycen), halves(ybuf), pw(0), ALU.subtract))
                if name == "var":
                    act("std")
                    done("inv2", V.reciprocal(ysq, ysq))
                    done("y1", V.tensor_tensor(ycen, ycen, ysq, ALU.mult))
                    done("y2", V.tensor_scalar(ycen, ycen, feat("lnw"), feat("lnb"), ALU.mult, ALU.add))
                    done("y3", V.tensor_tensor(ycen, ycen, bonus[:], ALU.add))
                if name == "gate":
                    pe("gate")
                    done("y4", V.tensor_tensor(halves(bt[:]), halves(ycen), pw(0), ALU.mult))

            def conv(tile, n):
                if tile == 1:
                    dve.wait_ge(evacuated[0], at(free(T_PAIR), 3, j))
                    dve.wait_ge(quarter_used, at(Q_PAIR + 8, 24, j))
                    V.tensor_tensor(halves(cu[:, 2:T + 2]), pd(n), halves(cx[:]), ALU.mult).then_inc(evacuated[n % 2], 1)
                    dve.wait_ge(evacuated[1], at(free(n), 3, j))
                    tap = lambda w: par[:, bass.ds(j + (PAR["conv"] + 8 * w), 1)]
                    V.tensor_scalar(cx[:], cu[:, 0:T], tap(0), None, ALU.mult).then_inc(conv_step, 1)
                    for w in (1, 2):
                        dve.wait_ge(conv_step, at(w, 3, j))
                        V.scalar_tensor_tensor(cx[:], cu[:, w:T + w], tap(w), cx[:], ALU.mult,
                                               ALU.add).then_inc(conv_step, 1)
                if tile == 2:
                    dve.wait_ge(quarter_used, at(Q_PAIR + 12, 24, j))
                    dve.wait_ge(conv_step, at(3, 3, j))
                    V.tensor_tensor(halves(cx[:]), pd(n), halves(cx[:]), ALU.mult).then_inc(evacuated[n % 2], 1)

            splits, tiles, y_split = 0, 0, 0
            for i, (name, k) in enumerate(zip(PE_STEPS, schedule(last))):
                steps_of(name)
                while splits < k // KQ:
                    split(Q_PAIR + LEAD + splits, 24, j)
                    splits += 1
                while 16 * (tiles + 1) <= k:
                    n = T_PAIR + tiles
                    if tiles < 3:
                        conv(tiles, n)
                    else:
                        shift(n, (zr, zk, zv)[tiles - 3][:],
                              par[:, bass.ds(j + (PAR["mu"] + 8 * (tiles - 3) + 1), 1)], 3, j)
                    tiles += 1
                if last and i >= Y_FROM and y_split < KT - 1:
                    split_y(y_split)
                    y_split += 1
            assert n_done[0] == len(DVE_STEPS)

        dve.sem_inc(dve_done, 1)
        with dve.Fori(0, PAIRS - 1) as j:
            pair(j)
        pair(PAIRS - 1, last=True)
        split_y(KT - 1)

        dve.wait_ge(res_loaded, 16)
        with dve.Fori(0, KT // 2) as i:
            for e in range(2):
                for q in range(4 * e, 4 * e + 4):
                    split(Q_OUT + LEAD + q, 8, i)
                n = T_OUT + e
                dve.wait_ge(quarter_used, at(Q_OUT + 4 * (e + 1), 8, i))
                r = res[:, bass.ds(i * 2 + e, 1), :].rearrange("p k (a n) -> p (k a) n", a=2)
                V.tensor_tensor(r, pd(n), r, ALU.add).then_inc(evacuated[n % 2], 1)
        norm(1)

        def mlp_group(g, last=False):
            for m in range(UT):
                for a in range(4):
                    split(Q_MLP + LEAD + 4 * m + a, 64, g)
                n = T_MLP + m
                dve.wait_ge(evacuated[n % 2], at(free(n), 12, g))
                V.tensor_tensor(nt1[:, m % 3, :], nt1[:, m % 3, :], nt1[:, m % 3, :], ALU.mult).then_inc(u_sq, 1)
                dve.wait_ge(u_hi_ready, at(m + 1, UT, g))
                V.tensor_tensor(u_lo[:, m, :], nt1[:, m % 3, :], u_hi[:, m, :].bitcast(F32),
                                ALU.subtract).then_inc(u_ready, 1)
            for m in range(KT):
                for a in range(2):
                    q = 4 * UT + 2 * m + a
                    if q < 64 - (LEAD if last else 0):
                        split(Q_MLP + LEAD + q, 64, g)
                n = T_MLP + UT + m
                dve.wait_ge(quarter_used, at(Q_MLP + 4 * UT + 2 * (m + 1), 64, g))
                V.tensor_tensor(halves(res[:, m, :]), pd(n), halves(res[:, m, :]), ALU.add).then_inc(evacuated[n % 2], 1)

        with dve.Fori(0, FFG - 1) as g:
            mlp_group(g)
        mlp_group(FFG - 1, last=True)
        norm(2)
        for b in range(0, 16, 2):
            dve.wait_ge(fin_turned, b + 1)
            if b > 3:
                dve.wait_ge(rows_stored, 16 * (b // 4))
            V.tensor_copy(rows[:, (b % 4) * 512:(b % 4 + 1) * 512], xbank(b)).then_inc(fin_kept[0], 1)

    @block.tensor
    def _(pe):
        M = nc.tensor.matmul
        pe.wait_ge(consts_made, N_CONST)
        for b in range(17):
            if b % 4 == 1 or b == 0:
                pe.wait_ge(x_loaded[(b + 3) // 4], 16)
            if b >= 8:
                pe.wait_ge(x_kept[b % 2], (b - 8) // 2 + 1)
            if b == 0:
                for k in range(KT):
                    ins = nc.tensor.transpose(xbank(0)[:, k * META:(k + 1) * META], meta_rows[:, k * P:(k + 1) * P],
                                              ident[0:META, 0:META])
            else:
                t, k4 = divmod(b - 1, 4)
                for k in range(4):
                    ins = nc.tensor.transpose(xbank(b)[:, k * P:(k + 1) * P],
                                              x_rows[:, t, (4 * k4 + k) * P:(4 * k4 + k + 1) * P], ident[:])
            ins.then_inc(x_turned, 1)
        pe.wait_ge(x_kept[0], 9)
        pe.wait_ge(x_kept[1], 8)

        def sum_squares(i):
            sq = NORM[i][1]
            for k in range(KT):
                pe.wait_ge(squared, KT * i + k + 1)
                for a in range(2):
                    ins = M(PW[:, a, 0:HALF], ones[:], sq[:, k % 2, a * HALF:(a + 1) * HALF], start=(k == 0),
                            stop=(k == KT - 1))
                ins.then_inc(summed, 1)

        sum_squares(0)

        def dense(tiles, ktiles, q0, n0, hi, lo, per_q=0, per_n=0, it=0, operand=None):
            step_ = 0
            for t in range(tiles):
                n = n0 + t
                if n >= 2:
                    pe.wait_ge(evacuated[n % 2], at(free(n) - 1, per_n // 2, it))
                for k in range(ktiles):
                    q = q0 + step_ // KQ
                    if step_ % KQ == 0:
                        pe.wait_ge(lo_split, at(q + 1, per_q, it))
                    if t == 0 and operand:
                        operand(k)
                    whi, wlo = w_hi[:, q % RING, step_ % KQ, :], w_lo[:, q % RING, step_ % KQ, :]
                    for i, (w, v) in enumerate(((whi, hi), (whi, lo), (wlo, hi))):
                        for a in range(2):
                            ins = M(PD[:, 2 * (n % 2) + a, 0:HALF], w, v[:, k, a * HALF:(a + 1) * HALF],
                                    start=(k == 0 and i == 0), stop=(k == ktiles - 1 and i == 2))
                    step_ += 1
                    if step_ % KQ == 0:
                        ins.then_inc(quarter_used, 1)
                    yield

        for _ in dense(6, KT, Q_LOW, T_LOW, act_hi, act_lo, operand=lambda k: pe.wait_ge(act_ready, k + 1)):
            pass
        pe.wait_ge(low_done, 3)

        def pair(j, last=False):
            n_done = [0]

            def done(name, ins):
                assert PE_STEPS[n_done[0]] == name
                n_done[0] += 1
                ins.then_inc(pe_done, 1)

            act = lambda name: pe.wait_ge(act_done, step(ACT_STEPS, name, j))
            dve = lambda name: pe.wait_ge(dve_done, step(DVE_STEPS, name, j))
            pool = lambda name: pe.wait_ge(pool_done, step(POOL_STEPS, name, j))
            half = lambda ap, a: ap[:, a * HALF:(a + 1) * HALF]
            hc = [(h, c) for h in range(2) for c in range(NCH)]
            hs = [slice(0, HS), slice(HS, P)]

            def turn(bank, src):
                for c in range(NCH):
                    ins = nc.tensor.transpose(PW[0:C, bank + c // 3, c % 3 * P:(c % 3 + 1) * P], src(c), ident[:])
                return ins

            def steps_of(name):
                if name == "ss":
                    act("sq")
                    for a in range(2):
                        ins = M(PW[:, 2 + a, 0:HALF], same_head[:], half(fsq, a), start=True, stop=True)
                if name == "low":
                    pe.wait_ge(wa_loaded, at(32, 32, j))
                    dve("ssm")
                    for h in range(2):
                        for a in range(2):
                            ins = M(PW[:, 2 * h + a, 0:HALF], wa_w[hs[h], :], half(low_wa[hs[h], :], a), start=True, stop=True)
                if name == "vtr":
                    act("sigw")
                    ins = turn(0, lambda c: zv[:, c * C:(c + 1) * C])
                if name == "bsum":
                    dve("rb")
                    for a in range(2):
                        ins = M(PW[:, 2 + a, 0:HALF], same_head[:], half(ld, a), start=True, stop=True)
                if name == "atr":
                    dve("bon")
                    ins = turn(2, lambda c: ar[:, c, 0, :])
                if name == "btr":
                    dve("bt")
                    act("vtok")
                    ins = turn(0, lambda c: bt[:, c * C:(c + 1) * C])
                if name == "ktr":
                    dve("kt")
                    act("atok")
                    ins = turn(2, lambda c: kt[:, c * C:(c + 1) * C])
                if name[:4] == "gram":
                    r = int(name[4])
                    if r == 0:
                        dve("btok")
                        act("ktok")
                    for i in range(4 * r, 4 * r + 4):
                        if r:
                            dve(f"gram{i - 4}")
                        h, c2 = divmod(i % 6, 3)
                        for e in range(2):
                            c = 2 * c2 + e
                            ins = M(PW[0:C, i % 4, e * 2 * C:(e + 1) * 2 * C],
                                    (bt if i < 6 else kt)[hs[h], c * C:(c + 1) * C],
                                    ar[hs[h], c, :, :].rearrange("p s n -> p (s n)"), start=True, stop=True)
                if name == "mv":
                    dve("gram11")
                    act("vtok")
                    for h, c in hc:
                        ins = M(PW[0:C, h, c * HS:(c + 1) * HS], KA[:, h, c, 0, 0:C], v_tok[:, c, hs[h]], start=True, stop=True)
                if name == "x1":
                    pool("nm1")
                    for h, c in hc:
                        w = wide(EVEN[1])
                        ins = M(packed(PW[0:C, 2 + h, c * w:(c + 1) * w], EVEN[1], False), NM[:, h, c, 0:C],
                                multiplied(ident[0:C, :], EVEN[1]), start=True, stop=True)
                elif name[0] == "x":
                    m, h = int(name[1:-1]), "ab".index(name[-1])
                    pool(f"nm{m}")
                    if m == 2:
                        act("mv")
                        dve("t1")
                    else:
                        dve(f"t{m // 2}{'ab'[h]}")
                    w, bank = wide(EVEN[m]), banks(m, "x") + h
                    for c in range(NCH):
                        ins = M(packed(PW[0:C, bank, c * w:(c + 1) * w], EVEN[m], False), NM[:, h, c, 0:C],
                                multiplied(TM[:, h, c, :], EVEN[m]), start=True, stop=True)
                if name[0] == "t" and name[-1] in "ab":
                    what = name[:2] if name[1] == "t" else "t"
                    m, h = int(name[len(what):-1]), "ab".index(name[-1])
                    if m > 2:
                        dve(f"tt{m // 2}{'ab'[h]}")
                    else:
                        pool("tt0")
                    act(f"x{m}{'ab'[h]}")
                    pool(f"xz{m}")
                    which, bank = (EVEN if what == "t" else ODD)[m], banks(m, what) + h
                    w = wide(which)
                    for c in range(NCH):
                        o = packed(PW[0:C, bank, c * w:(c + 1) * w], which, False)
                        if what == "t":
                            ins = M(o, TTM[:, h, c, 0:C], multiplied(XM[:, h, c, :], which), start=True, stop=True)
                        else:
                            ins = M(o, XM[:, h, c, 0:C], multiplied(TTM[:, h, c, :], which), start=True, stop=True)
                if name == "pq":
                    dve("tt64b")
                    for i, (h, c) in enumerate(hc):
                        ins = M(PW[0:C, i // 4, i % 4 * P:(i % 4 + 1) * P], TTM[:, h, c, 0:C], AMV[:, h, c, :], start=True, stop=True)
                if name == "gh":
                    act("pq")
                    for h in range(2):
                        for c in range(1, NCH - 1):
                            M(PW[hs[h], 0, (c - 1) * HS:c * HS], PQ[:, h, c, 0:HS], b_tok[:, c, hs[h]], start=True, stop=True)
                        for c in range(NCH - 1):
                            o = PW[hs[h], 1, c * HS:(c + 1) * HS]
                            M(o, b_tok[:, c, hs[h]], PQ[:, h, c, HS:P], start=True, stop=False)
                            ins = M(o, k_tok[:, c, hs[h]], v_tok[:, c, hs[h]], start=False, stop=True)
                if name == "e":
                    for h in range(2):
                        for c in range(1, NCH):
                            ins = M(PW[hs[h], 2, (c - 1) * C:c * C], PQ[:, h, c, 0:HS], NA[:, h, c, 1, 0:C], start=True, stop=True)
                if name in ("z2", "z3", "z4", "z5"):
                    c = int(name[1]) - 1
                    dve("hb" if c == 1 else f"z{c}")
                    ins = M(PW[:, (c - 1) % 2, 0:P], GT[:, c - 1, :], HB[:, 0, :] if c == 1 else ZB[:, c - 2, :],
                            start=True, stop=True)
                if name == "y":
                    dve("e")
                    dve("z5")
                    for c in range(NCH):
                        o = PW[:, 2 + c // 3, c % 3 * C:(c % 3 + 1) * C]
                        for h in range(2):
                            if c:
                                M(o[hs[h]], (HB[hs[h], 0, :] if c == 1 else ZB[hs[h], c - 2, :])[:, hs[h]],
                                  ET[hs[h], c - 1, :], start=True, stop=False, skip_group_check=True)
                            M(o[hs[h]], PQ[:, h, c, HS:P], NA[:, h, c, 1, 0:C], start=(c == 0), stop=False, skip_group_check=True)
                            ins = M(o[hs[h]], v_tok[:, c, hs[h]], KA[:, h, c, 1, 0:C], start=False, stop=True, skip_group_check=True)
                if name == "mean":
                    act("y")
                    for a in range(2):
                        ins = M(PW[:, a, 0:HALF], head_mean[:], half(ybuf, a), start=True, stop=True)
                if name == "var":
                    act("sqc")
                    for a in range(2):
                        ins = M(PW[:, 2 + a, 0:HALF], head_mean[:], half(ysq, a), start=True, stop=True)
                if name == "gate":
                    dve("yc")
                    pe.wait_ge(g_loaded, at(32, 32, j))
                    for a in range(2):
                        M(PW[:, a, 0:HALF], g_w[:], half(low_g[:], a), start=True, stop=False)
                        ins = M(PW[:, a, 0:HALF], g_w2[:], half(low_g2[:], a), start=False, stop=True)
                done(name, ins)

            projections = dense(3 if last else 6, KT, Q_PAIR, T_PAIR, act_hi, act_lo, 24, 6, j)
            k_steps = 0
            for name, k in zip(PE_STEPS, schedule(last)):
                while k_steps < k:
                    next(projections)
                    k_steps += 1
                steps_of(name)

        pe.sem_inc(pe_done, 1)
        with pe.Fori(0, PAIRS - 1) as j:
            pair(j)
        pair(PAIRS - 1, last=True)

        with pe.Fori(0, KT // 2) as i:
            for _ in dense(2, KT, Q_OUT, T_OUT, act_hi, act_lo, 8, 2, i, operand=lambda k: pe.wait_ge(y_ready, k + 1)):
                pass
        sum_squares(1)
        with pe.Fori(0, FFG) as g:
            for _ in dense(UT, KT, Q_MLP, T_MLP, act_hi, act_lo, 64, 24, g,
                           operand=lambda k: pe.wait_ge(act_ready, KT + k + 1)):
                pass
            for _ in dense(KT, UT, Q_MLP + 4 * UT, T_MLP + UT, u_hi, u_lo, 64, 24, g,
                           operand=lambda k: pe.wait_ge(u_ready, at(k + 1, UT, g))):
                pass
        sum_squares(2)
        pe.wait_ge(normed, 3 * KT)
        for b in range(16):
            if b >= 8:
                pe.wait_ge(fin_kept[b % 2], (b - 8) // 2 + 1)
            t, k4 = divmod(b, 4)
            for k in range(4):
                ins = nc.tensor.transpose(xbank(b)[:, k * P:(k + 1) * P],
                                          res[:, 4 * k4 + k, META + t * P:META + (t + 1) * P], ident[:])
            ins.then_inc(fin_turned, 1)

    ctx.close()


_INS = ["x", "meta_tokens", "norm_mix_g", "w_in", "shift_mu", "conv_w", "decay_w0", "decay_w2", "iclr_a0",
        "iclr_a2", "gate_g2", "k_k", "k_a", "r_k", "lnx_w", "lnx_b", "w_out", "norm_mlp_g", "w_up", "w_down",
        "final_norm_g"]


def kernel(**inputs):
    import numpy as _np
    import concourse.bacc as _bacc
    from concourse.bass_utils import run_bass_kernel_spmd as _run

    nc = _bacc.Bacc("TRN2", target_bir_lowering=False, num_devices=1)
    arrays, args = {}, []
    for name in _INS:
        a = _np.ascontiguousarray(inputs[name])
        if name not in ("meta_tokens", "final_norm_g"):
            a = a[0]
        if name == "r_k":
            a = a.reshape(-1)
        arrays[f"in_{name}"] = a
        args.append(nc.dram_tensor(f"in_{name}", a.shape, mybir.dt.from_np(a.dtype), kind="ExternalInput").ap())
    args.append(nc.dram_tensor("out_0", (SEQ, D), F32, kind="ExternalOutput").ap())
    hybrid_layer(nc, *args)
    r = _run(nc, [arrays], core_ids=[0])
    return r.results[0]["out_0"].reshape(1, SEQ, D)
```

```python
import math
from contextlib import ExitStack

import concourse.bass as bass
from concourse import mybir

F32 = mybir.dt.float32
F32R = mybir.dt.float32r
ALU = mybir.AluOpType
ACT = mybir.ActivationFunctionType

P = 128
D = 2048
KT = D // P
META = 16
SEQ = 512
T = META + SEQ
HALF = T // 2
DH = D // 2
PAIRS = DH // P
HS = 64
CONV = 3 * DH
LOWR = 2 * DH * 3
GATE_TAIL = 32
DFF = 4 * D
C = 88
NCH = T // C
CP = 96
MID = C // 2 - 1
LEVELS = [1, 2, 4, 8, 16, 32, 64]
NORM_EPS = 1e-5
LNX_EPS = 1e-5 * HS
KQ = 4
RAW = 4
RING = 8
LEAD = 4
FFG = DFF // 1024
UT = 1024 // P

ACC_STEPS = 1 + 2 * (KT - 1)

PE_STEPS = (["ss", "low", "vtr", "bsum", "atr", "btr", "ktr", "gram0", "gram1", "gram2", "mv", "x1"]
            + [f"{s}{m}{h}" for m in LEVELS[1:-1] for s in ("x", "t", "tt") for h in "ab"]
            + ["x64a", "x64b", "tt64a", "tt64b"]
            + ["pq", "gh", "e", "z2", "z3", "z4", "z5", "y", "mean", "var", "gate"])
ACT_STEPS = (["sq", "nrm", "sigw", "siga", "epv", "em", "ep", "gs", "vtok", "atok", "ktok", "mv"]
             + [f"x{m}{h}" for m in LEVELS[1:] for h in "ab"] + ["warm", "pq", "y", "sqc", "std"])
DVE_STEPS = (["kk", "ssm", "inv", "kkn", "ld", "scan", "mid", "mu", "epv", "gs", "tfac", "kp", "rb",
              "at", "b", "bt", "kt", "rt", "bon", "btok"] + [f"gram{i}" for i in range(12)]
             + ["t1"] + [f"{s}{m}{h}" for m in LEVELS[1:-1] for s in ("t", "tt") for h in "ab"] + ["tt64a", "tt64b"]
             + ["gt", "hb", "e", "z2", "z3", "z4", "z5", "yc", "inv2", "y1", "y2", "y3", "y4"])
POOL_STEPS = (["nm1", "tt0", "t0"] + [s for m in LEVELS[1:] for s in (f"nm{m}", f"xz{m}")])


def banks(m, what):
    first = 2 * (LEVELS.index(m) % 2)
    return {"x": 2 - first, "t": first, "tt": 2 - first}[what]


EVEN = {1: (22, 4, (0, 3), (0, 3, 2)), 2: (22, 4, (0, 3), (0, 2)), 4: (11, 8, (0, 6), (0, 4)),
        8: (6, 16, (0, 11), (0, 8)), 16: (3, 32, (0, 22), (0, 16)), 32: (1, 96, (0, 64), (0, 32)),
        64: (1, 96, (0, 64), (0, 64))}
ODD = {2: (22, 4, (1, 4), (2, 4)), 4: (11, 8, (2, 8), (4, 8)), 8: (6, 16, (5, 16), (8, 16)),
       16: (3, 32, (10, 32), (16, 32)), 32: (1, 96, (32, 96), (32, 64)),
       64: (1, 96, (32, 96), (64, 88))}
REST = {2: (22, 4, (2, 4)), 4: (11, 8, (4, 8)), 8: (6, 16, (8, 16)), 16: (3, 32, (16, 32)),
        32: (1, 96, (32, 96)), 64: (1, 96, (64, 96))}


def cut(ap, blocks, stride, part):
    d = ap.ndim
    v = ap[:, 0:blocks * stride] if d == 2 else ap[:, :, 0:blocks * stride]
    part = slice(*part)
    if blocks == 1:
        return v[:, part] if d == 2 else v[:, :, part]
    if d == 2:
        return v.rearrange("p (b s) -> p b s", s=stride)[:, :, part]
    return v.rearrange("p c (b s) -> p c b s", s=stride)[:, :, :, part]


def kept(ap, cols):
    return cut(ap, cols[0], cols[1], cols[3])


def multiplied(ap, cols):
    return cut(ap, cols[0], cols[1], cols[2])


def wide(cols):
    return cols[0] * (cols[2][1] - cols[2][0])


def packed(ap, cols, keep):
    n, lo = cols[2][1] - cols[2][0], cols[2][0]
    part = (cols[3][0] - lo, min(cols[3][1] - lo, n), *cols[3][2:]) if keep else (0, n)
    return cut(ap, cols[0], n, part)


def at(static, per=0, it=0):
    return it * per + static


def step(steps, name, it):
    return at(steps.index(name) + 2, len(steps), it)


def before(steps, it):
    return at(1, len(steps), it)


PACE = dict(ss=2, low=6, vtr=5, bsum=8, atr=5, btr=1, ktr=1, gram0=1, gram1=1, gram2=1, mv=4, x1=2, x2a=6, pq=3, gh=3,
            e=2, z2=3, z3=2, z4=2, z5=2, y=3, mean=3, var=4, gate=4)


def schedule(last):
    rest_ = 96 - sum(PACE.values())
    chain = [n for n in PE_STEPS if n not in PACE and n[-1] == "a"]
    pace, total = [], 0
    for n in PE_STEPS:
        if n in PACE:
            total += PACE[n]
        elif n in chain:
            i = chain.index(n)
            total += (i + 1) * rest_ // len(chain) - i * rest_ // len(chain)
        pace.append(total)
    assert total == 96
    return [min(k, 48) if last else k for k in pace]


SPLIT_FIRST = ("low", "vtr", "y", "mean", "var")

OUT_PACE = dict(pq=1, gh=2, z2=1, z3=1, z4=1, z5=1, mean=2, var=3, gate=3)
assert sum(OUT_PACE.values()) == KT - 1

Y_FROM = 33


PAR = {}
PAR_COLS = 0
for _name, _w in (("g_mix", KT), ("g_mlp", KT), ("g_fin", KT), ("mu", 24), ("mu_low", 3), ("mun", 24),
                  ("mun_low", 3), ("conv", 24), ("w0", 8), ("a0", 8), ("k_k", 8), ("k_a", 8),
                  ("nk_a", 8), ("r_k", 8), ("lnw", 8), ("lnb", 8)):
    PAR[_name] = PAR_COLS
    PAR_COLS += _w
N_PAR = 16 * 15

Q_LOW, T_LOW = 0, 0
Q_RKV0, T_RKV0 = 12, 3
Q_PAIR, T_PAIR = 24, 6
Q_OUT, T_OUT = 24 + 7 * 24 + 12, 6 + 7 * 6 + 3
Q_MLP, T_MLP = Q_OUT + 4 * KT, T_OUT + KT
T_END = T_MLP + FFG * 24
N_CONST = 5 + 12 + 2 + 7 + 2 + 1 + 4


def hybrid_layer(nc, x, meta, norm_mix_g, w_in, shift_mu, conv_w, decay_w0, decay_w2, iclr_a0, iclr_a2,
                 gate_g2, k_k, k_a, r_k, lnx_w, lnx_b, w_out, norm_mlp_g, w_up, w_down, final_norm_g, out):
    ctx = ExitStack()
    sb = lambda name, shape, dt=F32, on=ctx: on.enter_context(nc.sbuf_tensor(name, shape, dt))
    sem = lambda name: ctx.enter_context(nc.semaphore(name))

    res_dram = nc.dram_tensor("residual", [D, T], F32, kind="Internal").ap()
    y_dram = nc.dram_tensor("mixed", [D, T], F32, kind="Internal").ap()
    res_view = res_dram.rearrange("(k p) t -> p k t", p=P)
    y_view = y_dram.rearrange("(k p) t -> p k t", p=P)

    over_hi, over_lo = ExitStack(), ExitStack()
    rows = sb("rows", [P, 4, D], on=over_hi)
    over_hi.close()
    act_hi = sb("act_hi", [P, KT, T], F32R)
    x_sq = sb("x_sq", [P, D], on=over_lo)
    over_lo.close()
    act_lo = sb("act_lo", [P, KT, T], F32R)
    w_raw = sb("w_raw", [P, RAW, KQ, P])
    w_hi = sb("w_hi", [P, RING, KQ, P], F32R)
    w_lo = sb("w_lo", [P, RING, KQ, P], F32R)
    par = sb("par", [P, PAR_COLS])
    ident = sb("ident", [P, P])
    ones = sb("ones", [P, P])
    same_head = sb("same_head", [P, P])
    head_mean = sb("head_mean", [P, P])
    level_mask = sb("level_mask", [P, 7, CP])
    ident_pad = sb("ident_pad", [P, CP])
    zeros = sb("zeros", [P, 66])
    eps_t = sb("eps_t", [P, 2])
    gram_mask = sb("gram_mask", [P, 2, 2, C])

    pre = ExitStack()
    x_rows = sb("x_rows", [P, 4, D], on=pre)
    meta_rows = sb("meta_rows", [META, D], on=pre)
    res0 = sb("res0", [P, KT, T], on=pre)
    ss0 = sb("ss0", [P, 5], on=pre)
    rs_diag = sb("rs_diag", [P, 5, P], on=pre)
    rs0 = sb("rs0", [P, T], on=pre)
    nt0 = sb("nt0", [P, 3, T], on=pre)
    blocks = sb("blocks", [P, 6, P], on=pre)
    pre.close()

    mix = ExitStack()
    m_sb = lambda name, shape: sb(name, shape, on=mix)
    shifted = m_sb("shifted", [P, T + 1])
    keep = m_sb("keep", [P, T])
    zr, zk, zv = (m_sb(n, [P, T]) for n in ("zr", "zk", "zv"))
    cx = m_sb("cx", [P, T])
    cu = m_sb("cu", [P, T + 2])
    low_wa = m_sb("low_wa", [P, T])
    low_g = m_sb("low_g", [P, T])
    low_g2 = m_sb("low_g2", [GATE_TAIL, T])
    wa_w = m_sb("wa_w", [P, P])
    g_w = m_sb("g_w", [P, P])
    g_w2 = m_sb("g_w2", [GATE_TAIL, P])
    ones_c = ones[:, 0:C]
    ar = m_sb("ar", [P, NCH, 2, C])
    bt = m_sb("bt", [P, T])
    kt = m_sb("kt", [P, T])
    bonus = m_sb("bonus", [P, T])
    NA = m_sb("NA", [C, 2, NCH, 2, CP])
    KA = m_sb("KA", [C, 2, NCH, 2, CP])
    AMV = m_sb("AMV", [C, 2, NCH, P])
    v_tok = m_sb("v_tok", [C, NCH, P])
    b_tok = m_sb("b_tok", [C, NCH, P])
    k_tok = m_sb("k_tok", [C, NCH, P])
    GT = m_sb("GT", [P, 4, P])
    HB = m_sb("HB", [P, 5, P])
    ZB = m_sb("ZB", [P, 4, P])
    mid = m_sb("mid", [P, NCH])
    gs = m_sb("gs", [P, 5])
    warm = m_sb("warm", [P, 1])
    uni = m_sb("uni", [P, 9 * T])
    ld, mu, ep, em, epv, asig, kk, kp, fsq = (uni[:, i * T:(i + 1) * T] for i in range(9))
    W = NCH * CP
    TM, XM, TTM, NM = (uni[0:C, 2 * i * W:2 * (i + 1) * W].rearrange("p (h c n) -> p h c n", h=2, c=NCH)
                       for i in range(4))
    PQ = uni[0:C, 0:12 * P].rearrange("p (h c n) -> p h c n", h=2, c=NCH)
    ybuf, ycen = uni[:, 4 * W:4 * W + T], uni[:, 4 * W + T:4 * W + 2 * T]
    ET = uni[:, 6 * W:6 * W + 5 * C].rearrange("p (c n) -> p c n", c=5)
    ysq = uni[:, 0:T]
    mix.close()

    post = ExitStack()
    u_hi = sb("u_hi", [P, UT, T], F32R, on=post)
    u_lo = sb("u_lo", [P, UT, T], F32R, on=post)
    res = sb("res", [P, KT, T], on=post)
    acc = sb("acc", [P, T], on=post)
    psq = sb("psq", [P, T], on=post)
    sq_last = sb("sq_last", [P, T], on=post)
    rs1 = sb("rs1", [P, T], on=post)
    nt1 = sb("nt1", [P, 3, T], on=post)
    rs_tok = sb("rs_tok", [P, 4], on=post)
    post.close()
    yin = ctx.enter_context(nc.sbuf_tensor("yin", [P, 2, T], F32))

    PD = ctx.enter_context(nc.psum_tensor("PD", [P, 4, 512], F32))
    PW = ctx.enter_context(nc.psum_tensor("PW", [P, 4, 512], F32))

    x_loaded = [sem(f"x_loaded{i}") for i in range(5)]
    par_loaded, gain_loaded = sem("par_loaded"), sem("gain_loaded")
    consts_made = sem("consts_made")
    par_derived = sem("par_derived")
    x_turned = sem("x_turned")
    x_kept = [sem("x_kept_dve"), sem("x_kept_act")]
    raw_loaded = [sem(f"raw_loaded{i}") for i in range(RAW)]
    raw_zeroed = sem("raw_zeroed")
    hi_split = sem("hi_split")
    lo_split = sem("lo_split")
    quarter_used = sem("quarter_used")
    evacuated = [sem("evacuated0"), sem("evacuated1")]
    x_squared, x_rooted, x_inverted = sem("x_squared"), sem("x_rooted"), sem("x_inverted")
    diag_made, rs_spread, rs0_kept = sem("diag_made"), sem("rs_spread"), sem("rs0_kept")
    normed, normed_by_pool = sem("normed"), sem("normed_by_pool")
    acc_step, last_squared = sem("acc_step"), sem("last_squared")
    summed, rooted, rs_ready = sem("summed"), sem("rooted"), sem("rs_ready")
    act_hi_ready = sem("act_hi_ready")
    act_ready = sem("act_ready")
    res_loaded = [sem("res_loaded_first"), sem("res_loaded_rest")]
    pe_done, act_done, dve_done, pool_done = (sem(f"pair_steps_{e}") for e in ("pe", "act", "dve", "pool"))
    wa_loaded, g_loaded = sem("wa_loaded"), sem("g_loaded")
    low_done = sem("low_done")
    z_done = sem("z_done")
    conv_step = sem("conv_step")
    conv_stored, y_stored = sem("conv_stored"), sem("y_stored")
    zeroed = sem("zeroed")
    y_loaded = [sem("y_loaded0"), sem("y_loaded1")]
    y_hi, y_ready = sem("y_hi"), sem("y_ready")
    u_sq, u_hi_ready, u_ready = sem("u_sq"), sem("u_hi_ready"), sem("u_ready")
    gained, fin_turned, fin_kept = sem("gained"), sem("fin_turned"), sem("fin_kept")
    rows_scaled = [sem("rows_scaled_dve"), sem("rows_scaled_act")]
    rows_stored = sem("rows_stored")

    def p_(name, i, n=1):
        return par[:, PAR[name] + i:PAR[name] + i + n]

    def halves(ap):
        return ap.rearrange("p (a n) -> p a n", a=2)

    def pd(n):
        return PD[:, 2 * (n % 2):2 * (n % 2) + 2, 0:HALF]

    def pw(b):
        return PW[:, b:b + 2, 0:HALF]

    def xbank(b):
        return (PD if b % 8 < 4 else PW)[:, b % 4, :]

    def free(n):
        return n // 2 + 1

    win_q = w_in.rearrange("(a k p) n -> a p k n", k=KQ, p=P)
    conv_q = win_q[:, :, :, 0:CONV].rearrange("a p k (s m n) -> a p k s m n", s=3, n=P)
    rkv_q = win_q[:, :, :, CONV:LOWR].rearrange("a p k (s m n) -> a p k s m n", s=3, n=P)
    wout_q = w_out.rearrange("(a k p) (m n) -> a p k m n", k=KQ, p=P, n=P)
    wup_q = w_up.rearrange("(a k p) (g m n) -> a p k g m n", k=KQ, p=P, g=FFG, n=P)
    wdn_q = w_down.rearrange("(g a k p) (m n) -> g a p k m n", g=FFG, k=KQ, p=P, n=P)

    RS_CUT = META + 3 * P
    T_LAST = T_MLP + 24 * (FFG - 1) + UT

    block = ctx.enter_context(nc.Block())

    @block.sync
    def _(sp):
        sp.dma_start(meta_rows[:], meta).then_inc(x_loaded[0], 16)
        for i in range(4):
            sp.dma_start(x_rows[:, i, :], x[i * P:(i + 1) * P, :]).then_inc(x_loaded[i + 1], 16)

        def load(src, q, per=0, it=0, width=P):
            if q >= RAW:
                sp.wait_ge(lo_split, at(q - RAW + 1, per, it))
            sp.dma_start(w_raw[:, q % RAW, :, 0:width], src).then_inc(raw_loaded[q % RAW], 16)

        fm = lambda p: p.rearrange("(t p) -> p t", p=P)
        sp.dma_start(p_("g_mix", 0, KT), fm(norm_mix_g), allow_slow_non_contiguous=True).then_inc(gain_loaded, 16)

        def load_parameters():
            n_par = 0
            for name, src in (("g_mlp", fm(norm_mlp_g)), ("g_fin", fm(final_norm_g)),
                              ("mu", fm(shift_mu[0:3 * DH])), ("mu_low", fm(shift_mu[3 * DH:3 * DH + 2 * P])),
                              ("w0", fm(decay_w0)), ("a0", fm(iclr_a0)), ("k_k", fm(k_k)), ("k_a", fm(k_a)),
                              ("r_k", fm(r_k)),
                              ("lnw", fm(lnx_w)), ("lnb", fm(lnx_b))):
                sp.dma_start(par[:, PAR[name]:PAR[name] + src.shape[1]], src, allow_slow_non_contiguous=True).then_inc(par_loaded, 16)
                n_par += 16
            for w in range(3):
                sp.dma_start(p_("conv", 8 * w, 8), fm(conv_w[w]), allow_slow_non_contiguous=True).then_inc(par_loaded, 16)
                n_par += 16
            sp.dma_start(par[0:GATE_TAIL, PAR["mu_low"] + 2:PAR["mu_low"] + 3],
                          shift_mu[3 * DH + 2 * P:3 * DH + 2 * P + GATE_TAIL].rearrange("(p t) -> p t", t=1),
                          allow_slow_non_contiguous=True).then_inc(par_loaded, 16)
            n_par += 16
            assert n_par == N_PAR

        q = Q_LOW
        sp.wait_ge(raw_zeroed, 1)
        for first, width in ((LOWR + 2 * P, GATE_TAIL), (LOWR, P), (LOWR + P, P)):
            for a in range(4):
                load(win_q[a, :, :, first:first + width], q, width=width)
                q += 1
            if first == LOWR:
                load_parameters()
        for s in range(3):
            for a in range(4):
                load(rkv_q[a, :, :, s, 0, :], q)
                q += 1
        with sp.Fori(0, PAIRS - 1) as j:
            q = Q_PAIR
            for s in (0, 2, 1):
                for a in range(4):
                    load(conv_q[a, :, :, s, j, :], q, 24, j)
                    q += 1
            for s in range(3):
                for a in range(4):
                    load(rkv_q[a, :, :, s, j + 1, :], q, 24, j)
                    q += 1
        q = Q_PAIR + 7 * 24
        for s in (0, 2, 1):
            for a in range(4):
                load(conv_q[a, :, :, s, PAIRS - 1, :], q)
                q += 1
        def load_out(i):
            for n in range(2):
                for a in range(4):
                    load(wout_q[a, :, :, i * 2 + n, :], Q_OUT + 4 * n + a, 8, i)

        load_out(0)
        for k in range(KT - 1):
            if k < PAIRS:
                sp.wait_ge(conv_stored, 16 * (k + 2))
            else:
                sp.wait_ge(y_stored, 16 * (k - PAIRS + 2))
            if k >= 2:
                sp.wait_ge(y_ready, k - 1)
            sp.dma_start(yin[:, k % 2, :], y_view[:, k, :]).then_inc(y_loaded[k % 2], 16)
        with sp.Fori(1, KT // 2) as i:
            load_out(i)
        with sp.Fori(0, FFG) as g:
            for m in range(UT):
                for a in range(4):
                    load(wup_q[a, :, :, g, m, :], Q_MLP + 4 * m + a, 64, g)
            for m in range(KT):
                for a in range(2):
                    load(wdn_q[g, a, :, :, m, :], Q_MLP + 32 + 2 * m + a, 64, g)
        for t in range(4):
            for h in range(2):
                sp.wait_ge(rows_scaled[h], t + 1)
                sp.dma_start(out[t * P:(t + 1) * P, h * DH:(h + 1) * DH],
                             rows[:, t, h * DH:(h + 1) * DH]).then_inc(rows_stored, 16)
        sp.wait_ge(rows_stored, 16 * 8)

    @block.gpsimd
    def _(pool):
        made = [0]

        def const(ins, wait=True):
            made[0] += 1
            ins.then_inc(consts_made, 1)
            if wait:
                pool.wait_ge(consts_made, made[0])

        const(nc.gpsimd.memset(ident[:], 0.0))
        const(nc.gpsimd.affine_select(out=ident[:], in_=ident[:], compare_op=ALU.not_equal, fill=1.0, base=0,
                                      pattern=[[-1, P]], channel_multiplier=1))
        const(nc.gpsimd.memset(ones[:], 1.0))
        const(nc.gpsimd.memset(zeros[:], 0.0))
        const(nc.gpsimd.memset(blocks[:], 1.0))
        for i, m in enumerate(LEVELS[1:]):
            v = blocks[:, i, :].rearrange("p (b n) -> p b n", n=m)
            const(nc.gpsimd.affine_select(out=v, in_=v, compare_op=ALU.is_ge, fill=0.0, base=0,
                                          pattern=[[-m, P // m], [0, m]], channel_multiplier=1))
            const(nc.gpsimd.affine_select(out=v, in_=v, compare_op=ALU.is_ge, fill=0.0, base=m - 1,
                                          pattern=[[m, P // m], [0, m]], channel_multiplier=-1))
        const(nc.gpsimd.tensor_copy(ident_pad[:], ident[:, 0:CP]))
        const(nc.gpsimd.memset(ident_pad[:, C:CP], 0.0))
        const(nc.gpsimd.tensor_tensor(level_mask[:, 0, :], blocks[:, 0, 0:CP], ident[:, 0:CP], ALU.subtract))
        for i in range(1, 6):
            const(nc.gpsimd.tensor_tensor(level_mask[:, i, :], blocks[:, i, 0:CP], blocks[:, i - 1, 0:CP], ALU.subtract))
        const(nc.gpsimd.tensor_tensor(level_mask[:, 6, :], ones[:, 0:CP], blocks[:, 5, 0:CP], ALU.subtract))
        const(nc.gpsimd.tensor_copy(same_head[:], blocks[:, 5, :]))
        const(nc.gpsimd.tensor_scalar(head_mean[:], blocks[:, 5, :], 1.0 / HS, None, ALU.mult))
        const(nc.gpsimd.memset(gram_mask[:], 1.0))
        for c in range(2):
            for strict in range(2):
                v = gram_mask[:, c, 1 - strict, :]
                const(nc.gpsimd.affine_select(out=v, in_=v, compare_op=ALU.is_ge, fill=0.0, base=-strict,
                                              pattern=[[1, C]], channel_multiplier=-1))

        pool.wait_ge(x_kept[0], 9)
        pool.wait_ge(x_kept[1], 8)
        pool.dma_start(res_view[:, 0:KT // 2, :], res0[:, 0:KT // 2, :]).then_inc(conv_stored, 16)
        pool.dma_start(res_view[:, KT // 2:KT, :], res0[:, KT // 2:KT, :]).then_inc(y_stored, 16)
        pool.wait_ge(rs0_kept, 2)
        for k in range(2, KT, 3):
            if k >= 3:
                pool.wait_ge(act_ready, k - 2)
            nc.gpsimd.tensor_tensor(nt0[:, 2, :], res0[:, k, :], rs0[:], ALU.mult).then_inc(normed_by_pool, 1)

        pool.wait_ge(act_ready, KT)
        pool.wait_ge(conv_stored, 16)
        pool.wait_ge(y_stored, 16)
        nc.gpsimd.memset(NA[:], 0.0)
        nc.gpsimd.memset(shifted[:, 0:1], 0.0)
        nc.gpsimd.memset(cu[:, 0:2], 0.0)
        nc.gpsimd.memset(GT[:], 0.0)
        nc.gpsimd.memset(HB[:], 0.0).then_inc(zeroed, 1)
        pool.wait_ge(zeroed, 1)
        pool.sem_inc(pool_done, 1)

        def load_wa(j):
            pool.dma_start(wa_w[0:HS, :], decay_w2[:, bass.ts(j, P)]).then_inc(wa_loaded, 16)
            pool.dma_start(wa_w[HS:P, :], iclr_a2[:, bass.ts(j, P)]).then_inc(wa_loaded, 16)

        def load_g(j):
            pool.dma_start(g_w[:], gate_g2[0:P, bass.ts(j, P)]).then_inc(g_loaded, 16)
            pool.dma_start(g_w2[:], gate_g2[P:P + GATE_TAIL, bass.ts(j, P)]).then_inc(g_loaded, 16)

        def pair(j, last=False):
            n = [0]

            def done(name, ins):
                assert POOL_STEPS[n[0]] == name
                n[0] += 1
                ins.then_inc(pool_done, 1)

            if not last:
                pool.wait_ge(pe_done, step(PE_STEPS, "low", j))
                load_wa(j + 1)

            def mask_n(i):
                m = LEVELS[i]
                nc_ = level_mask[0:C, i, :].unsqueeze(1).to_broadcast([C, NCH, CP])
                for h in range(2):
                    ins = nc.gpsimd.tensor_tensor(NM[:, h, :, :], NA[:, h, :, 0, :], nc_, ALU.mult)
                done(f"nm{m}", ins)

            idp = ident_pad[0:C, :].unsqueeze(1).to_broadcast([C, NCH, CP])
            pool.wait_ge(dve_done, step(DVE_STEPS, "gram5", j))
            pool.wait_ge(dve_done, step(DVE_STEPS, "btok", j))
            mask_n(0)
            pool.wait_ge(pool_done, step(POOL_STEPS, "nm1", j))
            for h in range(2):
                ins = nc.gpsimd.tensor_tensor(TTM[:, h, :, :], NM[:, h, :, :], idp, ALU.add)
            done("tt0", ins)
            for h in range(2):
                ins = nc.gpsimd.tensor_copy(TM[:, h, :, :], idp)
            done("t0", ins)
            for i, m in enumerate(LEVELS[1:], 1):
                pool.wait_ge(pe_done, step(PE_STEPS, "x1" if m == 2 else f"x{m // 2}b", j))
                if m == 2:
                    pool.wait_ge(pool_done, step(POOL_STEPS, "t0", j))
                mask_n(i)
                if m > 2:
                    pool.wait_ge(pe_done, step(PE_STEPS, f"tt{m // 2}b", j))
                blocks_, _, part = REST[m]
                w = part[1] - part[0]
                nil = cut(zeros[0:C, 0:blocks_ * w].unsqueeze(1).to_broadcast([C, NCH, blocks_ * w]), blocks_, w, (0, w))
                for h in range(2):
                    ins = nc.gpsimd.tensor_tensor(cut(XM[:, h, :, :], *REST[m]), nil, nil, ALU.mult)
                done(f"xz{m}", ins)
                if m == 32:
                    store_conv(j)
            if not last:
                pool.wait_ge(dve_done, step(DVE_STEPS, "y4", j))
                pool.dma_start(y_view[:, bass.ds(j + PAIRS, 1), :], bt[:].unsqueeze(1)).then_inc(y_stored, 16)
                load_g(j + 1)

        def store_conv(j):
            pool.wait_ge(evacuated[0], at(free(T_PAIR + 2), 3, j))
            pool.dma_start(y_view[:, bass.ds(j, 1), :], cx[:].unsqueeze(1)).then_inc(conv_stored, 16)

        load_wa(0)
        load_g(0)
        with pool.Fori(0, PAIRS - 1) as j:
            pair(j)
        pair(PAIRS - 1, last=True)
        pool.wait_ge(y_ready, KT)
        pool.dma_start(res[:, 0:2, :], res_view[:, 0:2, :]).then_inc(res_loaded[0], 16)
        pool.dma_start(res[:, 2:KT, :], res_view[:, 2:KT, :]).then_inc(res_loaded[1], 16)

        def squares(n0, steps_, again):
            if again:
                pool.wait_ge(summed, 1)
            nc.gpsimd.memset(acc[:], 0.0).then_inc(acc_step, 1)

            def tile(e, i):
                r = res[:, bass.ds(i * 2 + e, 1), :].rearrange("p k t -> p (k t)")
                pool.wait_ge(evacuated[(n0 + e) % 2], at(free(n0 + e), 1, i))
                pool.wait_ge(acc_step, at(steps_ + 1 + 2 * e, 4, i))
                nc.gpsimd.tensor_tensor(psq[:], r, r, ALU.mult).then_inc(acc_step, 1)
                pool.wait_ge(acc_step, at(steps_ + 2 + 2 * e, 4, i))
                nc.gpsimd.tensor_tensor(acc[:], acc[:], psq[:], ALU.add).then_inc(acc_step, 1)

            with pool.Fori(0, KT // 2 - 1) as i:
                tile(0, i)
                tile(1, i)
            tile(0, KT // 2 - 1)

        squares(T_OUT, 0, False)
        squares(T_LAST, ACC_STEPS, True)
        pool.wait_ge(conv_stored, 16 * (PAIRS + 1))
        pool.wait_ge(y_stored, 16 * PAIRS)

    @block.scalar
    def _(act):
        act.wait_ge(x_loaded[0], 16)
        nc.scalar.activation(x_sq[0:META, :], meta_rows[:], ACT.Square, accum_out=ss0[0:META, 4:5]).then_inc(x_squared, 1)
        for b in range(1, 17, 2):
            if b % 4 == 1:
                i = b // 4
                act.wait_ge(x_loaded[i + 1], 16)
                act.wait_ge(x_squared, i + 1)
                nc.scalar.activation(x_sq[:], x_rows[:, i, :], ACT.Square, accum_out=ss0[:, i:i + 1]).then_inc(x_squared, 1)
            act.wait_ge(x_turned, b + 1)
            t, k4 = divmod(b - 1, 4)
            nc.scalar.copy(res0[:, 4 * k4:4 * k4 + 4, META + P * t:META + P * (t + 1)],
                           xbank(b).rearrange("p (k n) -> p k n", k=4)).then_inc(x_kept[1], 1)
        act.wait_ge(x_squared, 5)
        nc.scalar.activation(ss0[0:META, 4:5], ss0[0:META, 4:5], ACT.Sqrt, bias=eps_t[0:META, 0:1],
                             scale=1.0 / D).then_inc(x_rooted, 1)
        nc.scalar.activation(ss0[:, 0:4], ss0[:, 0:4], ACT.Sqrt, bias=eps_t[:, 0:1], scale=1.0 / D).then_inc(x_rooted, 1)
        def split(q, per=0, it=0):
            act.wait_ge(raw_loaded[q % RAW], at(16 * (q // RAW + 1), 16 * per // RAW, it))
            if q >= RING:
                act.wait_ge(quarter_used, at(q - RING + 1, per, it))
            nc.scalar.copy(w_hi[:, q % RING], w_raw[:, q % RAW]).then_inc(hi_split, 1)

        for q in range(Q_LOW, Q_LOW + LEAD):
            split(q)
        act.wait_ge(rs_spread, 1)
        nc.scalar.copy(rs0[:, 0:RS_CUT], PW[:, 0, 0:RS_CUT]).then_inc(rs0_kept, 1)
        nc.scalar.copy(rs0[:, RS_CUT:T], PW[:, 1, 0:T - RS_CUT]).then_inc(rs0_kept, 1)
        for k in range(KT):
            if k % 3 == 2:
                act.wait_ge(normed_by_pool, k // 3 + 1)
            else:
                act.wait_ge(normed, k - k // 3 + 1)
            if k == 0:
                act.wait_ge(gain_loaded, 16)
            nc.scalar.activation(act_hi[:, k, :], nt0[:, k % 3, :], ACT.Copy, scale=p_("g_mix", k)).then_inc(act_hi_ready, 1)
            if k >= 9 and k % 2:
                split(Q_LOW + LEAD + (k - 9) // 2)

        def take_shifted(n, q_done, mun, per_q=0, it=0, z_before=None, rows_=P):
            act.wait_ge(quarter_used, at(q_done, per_q, it))
            if z_before is not None:
                act.wait_ge(z_done, z_before)
            nc.scalar.copy(halves(shifted[0:rows_, 1:T + 1]), pd(n)[0:rows_])
            nc.scalar.activation(halves(keep[0:rows_, :]), pd(n)[0:rows_], ACT.Copy, scale=mun).then_inc(evacuated[n % 2], 1)

        act.wait_ge(zeroed, 1)
        act.wait_ge(par_loaded, N_PAR)
        act.wait_ge(par_derived, 4)
        for n in range(6):
            mun = p_("mun_low", (2, 0, 1)[n]) if n < 3 else p_("mun", 8 * (n - 3))
            rows_ = P if n else GATE_TAIL
            take_shifted(n, 4 * (n + 1), mun[0:rows_], z_before=n if n else None, rows_=rows_)
            for q in range(4 * n + 8, 4 * n + 12):
                if q < Q_PAIR + LEAD:
                    split(q)
            if n == 0:
                act.wait_ge(z_done, 1)
                nc.scalar.activation(low_g2[:], low_g2[:], ACT.Sigmoid).then_inc(low_done, 1)
            if n == 1:
                act.wait_ge(z_done, 2)
                nc.scalar.activation(low_wa[0:HS, :], low_wa[0:HS, :], ACT.Tanh).then_inc(low_done, 1)
            if n == 2:
                act.wait_ge(z_done, 3)
                nc.scalar.activation(low_g[:], low_g[:], ACT.Sigmoid).then_inc(low_done, 1)

        def split_y(k):
            if k == 0:
                act.wait_ge(quarter_used, Q_OUT)
            if k < KT - 1:
                act.wait_ge(y_loaded[k % 2], 16 * (k // 2 + 1))
            else:
                act.wait_ge(dve_done, step(DVE_STEPS, "y4", PAIRS - 1))
            nc.scalar.copy(act_hi[:, k, :], yin[:, k % 2, :] if k < KT - 1 else bt[:]).then_inc(y_hi, 1)

        def pair(j, last=False):
            n_done = [0]

            def done(name, ins):
                assert ACT_STEPS[n_done[0]] == name, (name, ACT_STEPS[n_done[0]])
                n_done[0] += 1
                ins.then_inc(act_done, 1)
                own(name)

            pe = lambda name: act.wait_ge(pe_done, step(PE_STEPS, name, j))
            dve = lambda name: act.wait_ge(dve_done, step(DVE_STEPS, name, j))
            own = lambda name: act.wait_ge(act_done, step(ACT_STEPS, name, j))
            feat = lambda name, w=1: par[:, bass.ds(j + PAR[name], 1)]

            def steps_of(name):
                if name == "ss":
                    done("sq", nc.scalar.activation(fsq, zk[:], ACT.Square, scale=feat("k_k")))
                    dve("ssm")
                    done("nrm", nc.scalar.activation(fsq, fsq, ACT.Sqrt))
                if name == "low":
                    pe("low")
                    done("sigw", nc.scalar.activation(halves(ld), pw(0), ACT.Sigmoid, bias=feat("w0")))
                    done("siga", nc.scalar.activation(halves(asig), pw(2), ACT.Sigmoid, bias=feat("a0")))
                if name == "vtr":
                    dve("epv")
                    done("epv", nc.scalar.activation(epv, epv, ACT.Exp))
                    done("em", nc.scalar.activation(em, mu, ACT.Exp, scale=-1.0))
                    done("ep", nc.scalar.activation(ep, mu, ACT.Exp))
                    dve("gs")
                    done("gs", nc.scalar.activation(gs[:], gs[:], ACT.Exp))
                    pe("vtr")
                    done("vtok", nc.scalar.copy(v_tok[:].rearrange("p (a c) n -> p a (c n)", a=2), PW[0:C, 0:2, 0:384]))
                if name == "atr":
                    pe("atr")
                    for a in range(2):
                        ins = nc.scalar.copy(AMV[:, :, 3 * a:3 * a + 3, 0:HS].rearrange("p h c n -> p c h n"),
                                             PW[0:C, 2 + a, 0:384].rearrange("p (c h n) -> p c h n", c=3, h=2))
                    done("atok", ins)
                if name == "ktr":
                    pe("ktr")
                    done("ktok", nc.scalar.copy(k_tok[:].rearrange("p (a c) n -> p a (c n)", a=2), PW[0:C, 2:4, 0:384]))
                if name == "mv":
                    pe("mv")
                    for h in range(2):
                        ins = nc.scalar.copy(AMV[:, h, :, HS:P], PW[0:C, h, 0:384].rearrange("p (c n) -> p c n", c=NCH))
                    done("mv", ins)
                if name[0] == "x" and name != "x1":
                    m, h = int(name[1:-1]), "ab".index(name[-1])
                    pe(name)
                    w = wide(EVEN[m])
                    done(name, nc.scalar.copy(
                        kept(XM[:, h, :, :], EVEN[m]),
                        packed(PW[0:C, banks(m, "x") + h, 0:NCH * w].rearrange("p (c n) -> p c n", c=NCH), EVEN[m], True)))
                if name == "tt64b":
                    done("warm", nc.scalar.activation(warm[:], eps_t[:, 0:1], ACT.Sqrt))
                if name == "pq":
                    pe("pq")
                    done("pq", nc.scalar.copy(PQ.rearrange("p h c n -> p (h c n)"),
                                              PW[0:C, 0:3, :].rearrange("p a n -> p (a n)")))
                if name == "y":
                    pe("y")
                    done("y", nc.scalar.copy(halves(ybuf), pw(2)))
                if name == "mean":
                    dve("yc")
                    done("sqc", nc.scalar.activation(ysq, ycen, ACT.Square))
                if name == "var":
                    pe("var")
                    done("std", nc.scalar.activation(halves(ysq), pw(2), ACT.Sqrt, bias=eps_t[:, 1:2]))

            splits, tiles, y_split = 0, 0, 0
            for i, (name, k) in enumerate(zip(PE_STEPS, schedule(last))):
                if name not in SPLIT_FIRST:
                    steps_of(name)
                while splits < k // KQ:
                    split(Q_PAIR + LEAD + splits, 24, j)
                    splits += 1
                if name in SPLIT_FIRST:
                    steps_of(name)
                while 16 * (tiles + 1) <= k:
                    n = T_PAIR + tiles
                    if tiles == 0:
                        act.wait_ge(quarter_used, at(Q_PAIR + 4, 24, j))
                        act.wait_ge(conv_stored, at(16, 16, j))
                        nc.scalar.copy(halves(cx[:]), pd(n)).then_inc(evacuated[n % 2], 1)
                    if tiles >= 3:
                        take_shifted(n, Q_PAIR + 4 * (tiles + 1), par[:, bass.ds(j + (PAR["mun"] + 8 * (tiles - 3) + 1), 1)],
                                     24, j, z_before=at(6 + tiles - 3, 3, j))
                    tiles += 1
                if last and i >= Y_FROM and y_split < KT - 1:
                    split_y(y_split)
                    y_split += 1
            assert n_done[0] == len(ACT_STEPS) and (not last or y_split == KT - 1)

        act.sem_inc(act_done, 1)
        with act.Fori(0, PAIRS - 1) as j:
            pair(j)
        pair(PAIRS - 1, last=True)

        split_y(KT - 1)

        with act.Fori(0, KT // 2 - 1) as i:
            for q in range(8):
                split(Q_OUT + LEAD + q, 8, i)
        q = Q_MLP - 8
        for a in range(8):
            split(q + LEAD + a)
            if a >= 4:
                act.wait_ge(quarter_used, q + a + 1)
                for k in range(4 * (a - 4), 4 * (a - 3)):
                    act.wait_ge(evacuated[(T_OUT + k) % 2], free(T_OUT + k))
                    nc.scalar.activation(act_hi[:, k, :], res[:, k, :], ACT.Copy, scale=p_("g_mlp", k)).then_inc(act_hi_ready, 1)
        for a in range(4):
            split(Q_MLP + LEAD + a)
        act.wait_ge(summed, 1)
        nc.scalar.activation(halves(rs1[:]), pw(0), ACT.Sqrt, bias=eps_t[:, 0:1], scale=1.0 / D).then_inc(rooted, 1)

        def mlp_group(g, last=False):
            n_split = [0]

            def splits(count):
                for _ in range(count):
                    if n_split[0] < 64 - (LEAD + 4 if last else 0):
                        split(Q_MLP + LEAD + 4 + n_split[0], 64, g)
                    n_split[0] += 1

            for m in range(UT):
                n = T_MLP + m
                act.wait_ge(evacuated[n % 2], at(free(n), 12, g))
                nt = nt1[:, m % 3, :]
                nc.scalar.activation(nt, nt, ACT.Square).then_inc(u_sq, 1)
                act.wait_ge(u_sq, at(m + 1, UT, g))
                nc.scalar.copy(u_hi[:, m, :], nt).then_inc(u_hi_ready, 1)
                splits(4)
            if not last:
                splits(2 * KT)
                return
            act.wait_ge(u_ready, UT * FFG)
            for m in range(KT):
                act.wait_ge(evacuated[(T_LAST + m) % 2], free(T_LAST + m))
                if m >= 3:
                    act.wait_ge(fin_turned, m - 2)
                nc.scalar.activation(nt1[:, m % 3, :], res[:, m, :], ACT.Copy, scale=p_("g_fin", m)).then_inc(gained, 1)
                splits(2)
                if m:
                    keep_rows(m - 1)
            keep_rows(KT - 1)

        def keep_rows(m):
            act.wait_ge(fin_turned, m + 1)
            nc.scalar.copy(rows[:, :, m * P:(m + 1) * P], PW[:, m % 4, :].rearrange("p (t n) -> p t n", t=4)).then_inc(fin_kept, 1)

        with act.Fori(0, FFG - 1) as g:
            mlp_group(g)
        mlp_group(FFG - 1, last=True)
        act.wait_ge(summed, 2)
        nc.scalar.activation(rs_tok[:], PW[:, 0, 0:4], ACT.Sqrt, bias=eps_t[:, 0:1], scale=1.0 / D).then_inc(rooted, 1)
        act.wait_ge(rs_ready, 2)
        for t in range(4):
            r = rows[:, t, DH:D]
            nc.scalar.activation(r, r, ACT.Copy, scale=rs_tok[:, t:t + 1]).then_inc(rows_scaled[1], 1)

    @block.vector
    def _(dve):
        V = nc.vector
        V.memset(w_raw[:, :, :, GATE_TAIL:P], 0.0).then_inc(raw_zeroed, 1)
        V.memset(eps_t[:, 0:1], NORM_EPS)
        V.memset(eps_t[:, 1:2], LNX_EPS)
        for b in range(0, 17, 2):
            dve.wait_ge(x_turned, b + 1)
            if b == 0:
                dst, src = res0[:, :, 0:META], xbank(0)[:, 0:KT * META].rearrange("p (k n) -> p k n", k=KT)
            else:
                t, k4 = divmod(b - 1, 4)
                dst = res0[:, 4 * k4:4 * k4 + 4, META + P * t:META + P * (t + 1)]
                src = xbank(b).rearrange("p (k n) -> p k n", k=4)
            V.tensor_copy(dst, src).then_inc(x_kept[0], 1)

        dve.wait_ge(x_rooted, 2)
        V.reciprocal(ss0[0:META, 4:5], ss0[0:META, 4:5]).then_inc(x_inverted, 1)
        V.reciprocal(ss0[:, 0:4], ss0[:, 0:4]).then_inc(x_inverted, 1)
        dve.wait_ge(x_inverted, 2)
        dve.wait_ge(consts_made, 2)
        V.tensor_scalar(rs_diag[0:META, 4, 0:META], ident[0:META, 0:META], ss0[0:META, 4:5], None, ALU.mult).then_inc(diag_made, 1)
        for i in range(4):
            V.tensor_scalar(rs_diag[:, i, :], ident[:], ss0[:, i:i + 1], None, ALU.mult).then_inc(diag_made, 1)

        def split(q, per=0, it=0):
            dve.wait_ge(hi_split, at(q + 1, per, it))
            V.tensor_tensor(w_lo[:, q % RING], w_raw[:, q % RAW], w_hi[:, q % RING].bitcast(F32),
                            ALU.subtract).then_inc(lo_split, 1)

        def low(k):
            dve.wait_ge(act_hi_ready, k + 1)
            V.scalar_tensor_tensor(act_lo[:, k, :], nt0[:, k % 3, :], p_("g_mix", k), act_hi[:, k, :].bitcast(F32),
                                   ALU.mult, ALU.subtract).then_inc(act_ready, 1)

        for q in range(Q_LOW, Q_LOW + LEAD):
            split(q)
        dve.wait_ge(x_kept[0], 9)
        dve.wait_ge(x_kept[1], 8)
        dve.wait_ge(rs0_kept, 2)
        dve.wait_ge(gain_loaded, 16)
        for k in range(KT):
            if k >= 3:
                dve.wait_ge(act_ready, k - 2)
            if k % 3 < 2:
                V.tensor_tensor(nt0[:, k % 3, :], res0[:, k, :], rs0[:], ALU.mult).then_inc(normed, 1)
            if k:
                low(k - 1)
            if k >= 10 and k % 2 == 0:
                split(Q_LOW + LEAD + (k - 10) // 2)
        low(KT - 1)
        split(Q_LOW + 2 * LEAD - 1)
        dve.wait_ge(par_loaded, N_PAR)
        one_minus = lambda o, i: V.tensor_scalar(o, i, -1.0, 1.0, ALU.mult, ALU.add)
        one_minus(p_("mun", 0, 24), p_("mu", 0, 24)).then_inc(par_derived, 1)
        one_minus(p_("mun_low", 0, 2), p_("mu_low", 0, 2)).then_inc(par_derived, 1)
        one_minus(p_("mun_low", 2)[0:GATE_TAIL], p_("mu_low", 2)[0:GATE_TAIL]).then_inc(par_derived, 1)
        one_minus(p_("nk_a", 0, 8), p_("k_a", 0, 8)).then_inc(par_derived, 1)

        def shift(n, dst, mu_, per=0, it=0, rows_=P):
            dve.wait_ge(evacuated[n % 2], at(free(n), per, it))
            V.scalar_tensor_tensor(dst, shifted[0:rows_, 0:T], mu_, keep[0:rows_, :], ALU.mult,
                                   ALU.add).then_inc(z_done, 1)

        dve.wait_ge(zeroed, 1)
        for n, dst in enumerate((low_g2, low_wa, low_g, zr, zk, zv)):
            m_ = p_("mu_low", (2, 0, 1)[n]) if n < 3 else p_("mu", 8 * (n - 3))
            rows_ = P if n else GATE_TAIL
            shift(n, dst[:], m_[0:rows_], rows_=rows_)
            for q in range(4 * n + 8, 4 * n + 12):
                if q < Q_PAIR + LEAD:
                    split(q)

        def split_y(k):
            dve.wait_ge(y_hi, k + 1)
            V.tensor_tensor(act_lo[:, k, :], yin[:, k % 2, :] if k < KT - 1 else bt[:],
                            act_hi[:, k, :].bitcast(F32), ALU.subtract).then_inc(y_ready, 1)

        def pair(j, last=False):
            n_done = [0]

            def done(name, ins):
                assert DVE_STEPS[n_done[0]] == name, (name, DVE_STEPS[n_done[0]])
                n_done[0] += 1
                ins.then_inc(dve_done, 1)
                own(name)

            pe = lambda name: dve.wait_ge(pe_done, step(PE_STEPS, name, j))
            act = lambda name: dve.wait_ge(act_done, step(ACT_STEPS, name, j))
            pool = lambda name: dve.wait_ge(pool_done, step(POOL_STEPS, name, j))
            own = lambda name: dve.wait_ge(dve_done, step(DVE_STEPS, name, j))
            feat = lambda name: par[:, bass.ds(j + PAR[name], 1)]
            chunks = lambda ap: ap.rearrange("p (c n) -> p c n", c=NCH)

            def steps_of(name):
                if name == "ss":
                    done("kk", V.tensor_scalar(kk, zk[:], feat("k_k"), None, ALU.mult))
                    pe("ss")
                    done("ssm", V.tensor_scalar(halves(fsq), pw(2), 1e-24, None, ALU.max))
                    act("nrm")
                    done("inv", V.reciprocal(fsq, fsq))
                    done("kkn", V.tensor_tensor(kk, kk, fsq, ALU.mult))
                if name == "low":
                    act("sigw")
                    done("ld", V.tensor_scalar(ld, ld, -math.exp(-0.5), None, ALU.mult))
                    for c in range(NCH):
                        ins = V.tensor_tensor_scan(mu[:, c * C:(c + 1) * C], ones_c, ld[:, c * C:(c + 1) * C],
                                                   0.0, ALU.mult, ALU.add)
                    done("scan", ins)
                    done("mid", V.tensor_copy(mid[:].unsqueeze(2), chunks(mu)[:, :, MID:MID + 1]))
                    done("mu", V.tensor_tensor(chunks(mu), chunks(mu), mid[:].unsqueeze(2).to_broadcast([P, NCH, C]),
                                               ALU.subtract))
                    done("epv", V.tensor_tensor(epv, mu, ld, ALU.subtract))
                    done("gs", V.tensor_tensor(gs[:].unsqueeze(2), chunks(mu)[:, 0:NCH - 1, C - 1:C],
                                               mid[:, 1:NCH].unsqueeze(2), ALU.add))
                if name == "vtr":
                    act("siga")
                    done("tfac", V.tensor_scalar(kp, asig, feat("k_a"), feat("nk_a"), ALU.mult, ALU.add))
                    done("kp", V.tensor_tensor(kp, zk[:], kp, ALU.mult))
                    done("rb", V.scalar_tensor_tensor(ld, zr[:], feat("r_k"), kp, ALU.mult, ALU.mult))
                    act("epv")
                    done("at", V.scalar_tensor_tensor(ar[:, :, 0, :], chunks(kk), -1.0, chunks(epv), ALU.mult, ALU.mult))
                    done("b", V.tensor_tensor(asig, kk, asig, ALU.mult))
                    act("em")
                    dve.wait_ge(y_stored, at(16, 16, j))
                    done("bt", V.tensor_tensor(bt[:], asig, em, ALU.mult))
                    done("kt", V.tensor_tensor(kt[:], kp, em, ALU.mult))
                    act("ep")
                    done("rt", V.tensor_tensor(ar[:, :, 1, :], chunks(zr[:]), chunks(ep), ALU.mult))
                if name == "bsum":
                    pe("bsum")
                    done("bon", V.tensor_tensor(halves(bonus[:]), pw(2), halves(zv[:]), ALU.mult))
                if name == "btr":
                    pe("btr")
                    done("btok", V.tensor_copy(b_tok[:].rearrange("p (a c) n -> p a (c n)", a=2), PW[0:C, 0:2, 0:384]))
                if name in ("gram0", "gram1", "gram2"):
                    pe(name)
                    for i in range(4 * int(name[4]), 4 * int(name[4]) + 4):
                        h, c2 = divmod(i % 6, 3)
                        done(f"gram{i}", V.tensor_tensor(
                            (NA if i < 6 else KA)[:, h, 2 * c2:2 * c2 + 2, :, 0:C],
                            PW[0:C, i % 4, 0:4 * C].rearrange("p (c s n) -> p c s n", c=2, s=2),
                            gram_mask[0:C], ALU.mult))

                def update(mat, which, bank, h):
                    n = wide(which)
                    dst = kept(mat[:, h, :, :], which)
                    src = packed(PW[0:C, bank + h, 0:NCH * n].rearrange("p (c n) -> p c n", c=NCH), which, True)
                    return V.tensor_tensor(dst, src, dst, ALU.add)

                if name == "x1":
                    pe("x1")
                    pool("t0")
                    update(TM, EVEN[1], 2, 0)
                    done("t1", update(TM, EVEN[1], 2, 1))
                if name[0] == "t" and name[-1] in "ab":
                    what = name[:2] if name[1] == "t" else "t"
                    m, h = int(name[len(what):-1]), "ab".index(name[-1])
                    pe(name)
                    if what == "t":
                        done(name, update(TM, EVEN[m], banks(m, "t"), h))
                    else:
                        done(name, update(TTM, ODD[m], banks(m, "tt"), h))
                if name == "gh":
                    pe("gh")
                    for h in range(2):
                        hs = slice(HS * h, HS * (h + 1))
                        ins = V.tensor_tensor(GT[hs, :, hs], PW[hs, 0, 0:4 * HS].rearrange("p (c n) -> p c n", c=4),
                                              ident[hs, hs].unsqueeze(1).to_broadcast([HS, 4, HS]), ALU.add)
                    done("gt", ins)
                    for h in range(2):
                        hs = slice(HS * h, HS * (h + 1))
                        ins = V.tensor_tensor(HB[hs, :, hs], PW[hs, 1, 0:5 * HS].rearrange("p (c n) -> p c n", c=5),
                                              gs[hs].unsqueeze(2).to_broadcast([HS, 5, HS]), ALU.mult)
                    done("hb", ins)
                if name == "e":
                    pe("e")
                    done("e", V.tensor_tensor(ET, PW[:, 2, 0:5 * C].rearrange("p (c n) -> p c n", c=5),
                                              ar[:, 1:NCH, 1, :], ALU.add))
                if name in ("z2", "z3", "z4", "z5"):
                    c = int(name[1]) - 1
                    pe(name)
                    done(name, V.scalar_tensor_tensor(ZB[:, c - 1, :], PW[:, (c - 1) % 2, 0:P], gs[:, c:c + 1],
                                                      HB[:, c, :], ALU.mult, ALU.add))
                if name == "mean":
                    pe("mean")
                    done("yc", V.tensor_tensor(halves(ycen), halves(ybuf), pw(0), ALU.subtract))
                if name == "var":
                    act("std")
                    done("inv2", V.reciprocal(ysq, ysq))
                    done("y1", V.tensor_tensor(ycen, ycen, ysq, ALU.mult))
                    done("y2", V.tensor_scalar(ycen, ycen, feat("lnw"), feat("lnb"), ALU.mult, ALU.add))
                    done("y3", V.tensor_tensor(ycen, ycen, bonus[:], ALU.add))
                if name == "gate":
                    pe("gate")
                    done("y4", V.tensor_tensor(halves(bt[:]), halves(ycen), pw(0), ALU.mult))

            def conv(tile, n):
                if tile == 1:
                    dve.wait_ge(evacuated[0], at(free(T_PAIR), 3, j))
                    dve.wait_ge(quarter_used, at(Q_PAIR + 8, 24, j))
                    V.tensor_tensor(halves(cu[:, 2:T + 2]), pd(n), halves(cx[:]), ALU.mult).then_inc(evacuated[n % 2], 1)
                    dve.wait_ge(evacuated[1], at(free(n), 3, j))
                    tap = lambda w: par[:, bass.ds(j + (PAR["conv"] + 8 * w), 1)]
                    V.tensor_scalar(cx[:], cu[:, 0:T], tap(0), None, ALU.mult).then_inc(conv_step, 1)
                    for w in (1, 2):
                        dve.wait_ge(conv_step, at(w, 3, j))
                        V.scalar_tensor_tensor(cx[:], cu[:, w:T + w], tap(w), cx[:], ALU.mult,
                                               ALU.add).then_inc(conv_step, 1)
                if tile == 2:
                    dve.wait_ge(quarter_used, at(Q_PAIR + 12, 24, j))
                    dve.wait_ge(conv_step, at(3, 3, j))
                    V.tensor_tensor(halves(cx[:]), pd(n), halves(cx[:]), ALU.mult).then_inc(evacuated[n % 2], 1)

            splits, tiles, y_split = 0, 0, 0
            for i, (name, k) in enumerate(zip(PE_STEPS, schedule(last))):
                if name not in SPLIT_FIRST:
                    steps_of(name)
                while splits < k // KQ:
                    split(Q_PAIR + LEAD + splits, 24, j)
                    splits += 1
                if name in SPLIT_FIRST:
                    steps_of(name)
                while 16 * (tiles + 1) <= k:
                    n = T_PAIR + tiles
                    if tiles < 3:
                        conv(tiles, n)
                    else:
                        shift(n, (zr, zk, zv)[tiles - 3][:],
                              par[:, bass.ds(j + (PAR["mu"] + 8 * (tiles - 3) + 1), 1)], 3, j)
                    tiles += 1
                if last and i >= Y_FROM and y_split < KT - 1:
                    split_y(y_split)
                    y_split += 1
            assert n_done[0] == len(DVE_STEPS)

        dve.sem_inc(dve_done, 1)
        with dve.Fori(0, PAIRS - 1) as j:
            pair(j)
        pair(PAIRS - 1, last=True)
        split_y(KT - 1)

        def add_out(e, i):
            n = T_OUT + e
            dve.wait_ge(quarter_used, at(Q_OUT + 4 * (e + 1), 8, i))
            r = res[:, bass.ds(i * 2 + e, 1), :].rearrange("p k (a n) -> p (k a) n", a=2)
            V.tensor_tensor(r, pd(n), r, ALU.add).then_inc(evacuated[n % 2], 1)

        def out_tiles(i):
            for e in range(2):
                for q in range(4 * e, 4 * e + 4):
                    split(Q_OUT + LEAD + q, 8, i)
                if e == 0 and isinstance(i, int):
                    dve.wait_ge(res_loaded[0], 16)
                add_out(e, i)

        out_tiles(0)
        dve.wait_ge(res_loaded[1], 16)
        with dve.Fori(1, KT // 2 - 1) as i:
            out_tiles(i)
        q = Q_MLP - 8
        for a in range(8):
            split(q + LEAD + a)
            if a == 3:
                add_out(0, KT // 2 - 1)
            if a == 7:
                add_out(1, KT // 2 - 1)
                dve.wait_ge(evacuated[(T_OUT + KT - 1) % 2], free(T_OUT + KT - 1))
                V.tensor_tensor(sq_last[:], res[:, KT - 1, :], res[:, KT - 1, :], ALU.mult).then_inc(last_squared, 1)
            if a >= 4:
                for k in range(4 * (a - 4), 4 * (a - 3)):
                    dve.wait_ge(act_hi_ready, KT + k + 1)
                    V.scalar_tensor_tensor(act_lo[:, k, :], res[:, k, :], p_("g_mlp", k), act_hi[:, k, :].bitcast(F32),
                                           ALU.mult, ALU.subtract).then_inc(act_ready, 1)
        for a in range(4):
            split(Q_MLP + LEAD + a)
        dve.wait_ge(rooted, 1)
        V.reciprocal(rs1[:], rs1[:]).then_inc(rs_ready, 1)
        dve.wait_ge(rs_ready, 1)

        def mlp_group(g, last=False):
            n_split = [0]

            def splits(count):
                for _ in range(count):
                    if n_split[0] < 64 - (LEAD + 4 if last else 0):
                        split(Q_MLP + LEAD + 4 + n_split[0], 64, g)
                    n_split[0] += 1

            def scale(m):
                n = T_MLP + m
                dve.wait_ge(quarter_used, at(Q_MLP + 4 * (m + 1), 64, g))
                if m >= 3:
                    dve.wait_ge(u_ready, at(m - 2, UT, g))
                V.scalar_tensor_tensor(halves(nt1[:, m % 3, :]), pd(n), 0.0, halves(rs1[:]), ALU.max,
                                       ALU.mult).then_inc(evacuated[n % 2], 1)

            def low(m):
                dve.wait_ge(u_hi_ready, at(m + 1, UT, g))
                V.tensor_tensor(u_lo[:, m, :], nt1[:, m % 3, :], u_hi[:, m, :].bitcast(F32),
                                ALU.subtract).then_inc(u_ready, 1)

            for m in range(UT):
                scale(m)
                splits(1)
                low(m)
                splits(3)
            for m in range(KT):
                n = T_MLP + UT + m
                dve.wait_ge(quarter_used, at(Q_MLP + 4 * UT + 2 * (m + 1), 64, g))
                V.tensor_tensor(halves(res[:, m, :]), pd(n), halves(res[:, m, :]), ALU.add).then_inc(evacuated[n % 2], 1)
                splits(2)

        with dve.Fori(0, FFG - 1) as g:
            mlp_group(g)
        mlp_group(FFG - 1, last=True)
        dve.wait_ge(evacuated[(T_END - 1) % 2], free(T_END - 1))
        V.tensor_tensor(sq_last[:], res[:, KT - 1, :], res[:, KT - 1, :], ALU.mult).then_inc(last_squared, 1)
        dve.wait_ge(rooted, 2)
        V.reciprocal(rs_tok[:], rs_tok[:]).then_inc(rs_ready, 1)
        dve.wait_ge(rs_ready, 2)
        dve.wait_ge(fin_kept, KT)
        for t in range(4):
            V.tensor_scalar(rows[:, t, 0:DH], rows[:, t, 0:DH], rs_tok[:, t:t + 1], None, ALU.mult).then_inc(rows_scaled[0], 1)

    @block.tensor
    def _(pe):
        M = nc.tensor.matmul
        pe.wait_ge(consts_made, 2)
        for b in range(17):
            if b % 4 == 1 or b == 0:
                pe.wait_ge(x_loaded[(b + 3) // 4], 16)
            if b >= 8:
                pe.wait_ge(x_kept[b % 2], (b - 8) // 2 + 1)
            if b == 0:
                for k in range(KT):
                    ins = nc.tensor.transpose(xbank(0)[:, k * META:(k + 1) * META], meta_rows[:, k * P:(k + 1) * P],
                                              ident[0:META, 0:META])
            else:
                t, k4 = divmod(b - 1, 4)
                for k in range(4):
                    ins = nc.tensor.transpose(xbank(b)[:, k * P:(k + 1) * P],
                                              x_rows[:, t, (4 * k4 + k) * P:(4 * k4 + k + 1) * P], ident[:])
            ins.then_inc(x_turned, 1)
        pe.wait_ge(x_kept[0], 9)
        pe.wait_ge(x_kept[1], 8)

        pe.wait_ge(consts_made, 3)
        pe.wait_ge(diag_made, 5)
        M(PW[:, 0, 0:META], ones[0:META, :], rs_diag[0:META, 4, 0:META], start=True, stop=True)
        for i in range(4):
            o = PW[:, 0, META + i * P:META + (i + 1) * P] if i < 3 else PW[:, 1, 0:P]
            ins = M(o, ones[:], rs_diag[:, i, :], start=True, stop=True)
        ins.then_inc(rs_spread, 1)

        def dense(tiles, ktiles, q0, n0, hi, lo, per_q=0, per_n=0, it=0, operand=None):
            step_ = 0
            for t in range(tiles):
                n = n0 + t
                if n >= 2:
                    pe.wait_ge(evacuated[n % 2], at(free(n) - 1, per_n // 2, it))
                for k in range(ktiles):
                    q = q0 + step_ // KQ
                    if step_ % KQ == 0:
                        pe.wait_ge(lo_split, at(q + 1, per_q, it))
                    if t == 0 and operand:
                        operand(k)
                    whi, wlo = w_hi[:, q % RING, step_ % KQ, :], w_lo[:, q % RING, step_ % KQ, :]
                    for i, (w, v) in enumerate(((whi, hi), (whi, lo), (wlo, hi))):
                        for a in range(2):
                            ins = M(PD[:, 2 * (n % 2) + a, 0:HALF], w, v[:, k, a * HALF:(a + 1) * HALF],
                                    start=(k == 0 and i == 0), stop=(k == ktiles - 1 and i == 2))
                    step_ += 1
                    if step_ % KQ == 0:
                        ins.then_inc(quarter_used, 1)
                    yield

        for _ in dense(6, KT, Q_LOW, T_LOW, act_hi, act_lo, operand=lambda k: pe.wait_ge(act_ready, k + 1)):
            pass
        pe.wait_ge(low_done, 3)
        pe.wait_ge(consts_made, N_CONST)

        def pair(j, last=False):
            n_done = [0]

            def done(name, ins):
                assert PE_STEPS[n_done[0]] == name
                n_done[0] += 1
                ins.then_inc(pe_done, 1)

            act = lambda name: pe.wait_ge(act_done, step(ACT_STEPS, name, j))
            dve = lambda name: pe.wait_ge(dve_done, step(DVE_STEPS, name, j))
            pool = lambda name: pe.wait_ge(pool_done, step(POOL_STEPS, name, j))
            half = lambda ap, a: ap[:, a * HALF:(a + 1) * HALF]
            hc = [(h, c) for h in range(2) for c in range(NCH)]
            hs = [slice(0, HS), slice(HS, P)]

            def turn(bank, src):
                for c in range(NCH):
                    ins = nc.tensor.transpose(PW[0:C, bank + c // 3, c % 3 * P:(c % 3 + 1) * P], src(c), ident[:])
                return ins

            def steps_of(name):
                if name == "ss":
                    act("sq")
                    for a in range(2):
                        ins = M(PW[:, 2 + a, 0:HALF], same_head[:], half(fsq, a), start=True, stop=True)
                if name == "low":
                    pe.wait_ge(wa_loaded, at(32, 32, j))
                    dve("ssm")
                    for h in range(2):
                        for a in range(2):
                            ins = M(PW[:, 2 * h + a, 0:HALF], wa_w[hs[h], :], half(low_wa[hs[h], :], a), start=True, stop=True)
                if name == "vtr":
                    act("sigw")
                    ins = turn(0, lambda c: zv[:, c * C:(c + 1) * C])
                if name == "bsum":
                    dve("rb")
                    for a in range(2):
                        ins = M(PW[:, 2 + a, 0:HALF], same_head[:], half(ld, a), start=True, stop=True)
                if name == "atr":
                    dve("bon")
                    ins = turn(2, lambda c: ar[:, c, 0, :])
                if name == "btr":
                    dve("bt")
                    act("vtok")
                    ins = turn(0, lambda c: bt[:, c * C:(c + 1) * C])
                if name == "ktr":
                    dve("kt")
                    act("atok")
                    ins = turn(2, lambda c: kt[:, c * C:(c + 1) * C])
                if name[:4] == "gram":
                    r = int(name[4])
                    if r == 0:
                        dve("btok")
                        act("ktok")
                    for i in range(4 * r, 4 * r + 4):
                        if r:
                            dve(f"gram{i - 4}")
                        h, c2 = divmod(i % 6, 3)
                        for e in range(2):
                            c = 2 * c2 + e
                            ins = M(PW[0:C, i % 4, e * 2 * C:(e + 1) * 2 * C],
                                    (bt if i < 6 else kt)[hs[h], c * C:(c + 1) * C],
                                    ar[hs[h], c, :, :].rearrange("p s n -> p (s n)"), start=True, stop=True)
                if name == "mv":
                    dve("gram11")
                    act("vtok")
                    for h, c in hc:
                        ins = M(PW[0:C, h, c * HS:(c + 1) * HS], KA[:, h, c, 0, 0:C], v_tok[:, c, hs[h]], start=True, stop=True)
                if name == "x1":
                    pool("nm1")
                    for h, c in hc:
                        w = wide(EVEN[1])
                        ins = M(packed(PW[0:C, 2 + h, c * w:(c + 1) * w], EVEN[1], False), NM[:, h, c, 0:C],
                                multiplied(ident[0:C, :], EVEN[1]), start=True, stop=True)
                elif name[0] == "x":
                    m, h = int(name[1:-1]), "ab".index(name[-1])
                    pool(f"nm{m}")
                    if m == 2:
                        act("mv")
                        dve("t1")
                    else:
                        dve(f"t{m // 2}{'ab'[h]}")
                    w, bank = wide(EVEN[m]), banks(m, "x") + h
                    for c in range(NCH):
                        ins = M(packed(PW[0:C, bank, c * w:(c + 1) * w], EVEN[m], False), NM[:, h, c, 0:C],
                                multiplied(TM[:, h, c, :], EVEN[m]), start=True, stop=True)
                if name[0] == "t" and name[-1] in "ab":
                    what = name[:2] if name[1] == "t" else "t"
                    m, h = int(name[len(what):-1]), "ab".index(name[-1])
                    if m > 2:
                        dve(f"tt{m // 2}{'ab'[h]}")
                    else:
                        pool("tt0")
                    act(f"x{m}{'ab'[h]}")
                    pool(f"xz{m}")
                    which, bank = (EVEN if what == "t" else ODD)[m], banks(m, what) + h
                    w = wide(which)
                    for c in range(NCH):
                        o = packed(PW[0:C, bank, c * w:(c + 1) * w], which, False)
                        if what == "t":
                            ins = M(o, TTM[:, h, c, 0:C], multiplied(XM[:, h, c, :], which), start=True, stop=True)
                        else:
                            ins = M(o, XM[:, h, c, 0:C], multiplied(TTM[:, h, c, :], which), start=True, stop=True)
                if name == "pq":
                    dve("tt64b")
                    for i, (h, c) in enumerate(hc):
                        ins = M(PW[0:C, i // 4, i % 4 * P:(i % 4 + 1) * P], TTM[:, h, c, 0:C], AMV[:, h, c, :], start=True, stop=True)
                if name == "gh":
                    act("pq")
                    for h in range(2):
                        for c in range(1, NCH - 1):
                            M(PW[hs[h], 0, (c - 1) * HS:c * HS], PQ[:, h, c, 0:HS], b_tok[:, c, hs[h]], start=True, stop=True)
                        for c in range(NCH - 1):
                            o = PW[hs[h], 1, c * HS:(c + 1) * HS]
                            M(o, b_tok[:, c, hs[h]], PQ[:, h, c, HS:P], start=True, stop=False)
                            ins = M(o, k_tok[:, c, hs[h]], v_tok[:, c, hs[h]], start=False, stop=True)
                if name == "e":
                    for h in range(2):
                        for c in range(1, NCH):
                            ins = M(PW[hs[h], 2, (c - 1) * C:c * C], PQ[:, h, c, 0:HS], NA[:, h, c, 1, 0:C], start=True, stop=True)
                if name in ("z2", "z3", "z4", "z5"):
                    c = int(name[1]) - 1
                    dve("hb" if c == 1 else f"z{c}")
                    ins = M(PW[:, (c - 1) % 2, 0:P], GT[:, c - 1, :], HB[:, 0, :] if c == 1 else ZB[:, c - 2, :],
                            start=True, stop=True)
                if name == "y":
                    dve("e")
                    dve("z5")
                    for c in range(NCH):
                        o = PW[:, 2 + c // 3, c % 3 * C:(c % 3 + 1) * C]
                        for h in range(2):
                            if c:
                                M(o[hs[h]], (HB[hs[h], 0, :] if c == 1 else ZB[hs[h], c - 2, :])[:, hs[h]],
                                  ET[hs[h], c - 1, :], start=True, stop=False, skip_group_check=True)
                            M(o[hs[h]], PQ[:, h, c, HS:P], NA[:, h, c, 1, 0:C], start=(c == 0), stop=False, skip_group_check=True)
                            ins = M(o[hs[h]], v_tok[:, c, hs[h]], KA[:, h, c, 1, 0:C], start=False, stop=True, skip_group_check=True)
                if name == "mean":
                    act("y")
                    for a in range(2):
                        ins = M(PW[:, a, 0:HALF], head_mean[:], half(ybuf, a), start=True, stop=True)
                if name == "var":
                    act("sqc")
                    for a in range(2):
                        ins = M(PW[:, 2 + a, 0:HALF], head_mean[:], half(ysq, a), start=True, stop=True)
                if name == "gate":
                    dve("yc")
                    pe.wait_ge(g_loaded, at(32, 32, j))
                    for a in range(2):
                        M(PW[:, a, 0:HALF], g_w[:], half(low_g[:], a), start=True, stop=False)
                        ins = M(PW[:, a, 0:HALF], g_w2[:], half(low_g2[:], a), start=False, stop=True)
                done(name, ins)

            projections = dense(3 if last else 6, KT, Q_PAIR, T_PAIR, act_hi, act_lo, 24, 6, j)
            k_steps = 0
            for name, k in zip(PE_STEPS, schedule(last)):
                while k_steps < k:
                    next(projections)
                    k_steps += 1
                for _ in range(OUT_PACE.get(name, 0) if last else 0):
                    next(first_out)
                steps_of(name)

        y_operand = lambda k: pe.wait_ge(y_ready, k + 1)
        first_out = dense(1, KT, Q_OUT, T_OUT, act_hi, act_lo, operand=y_operand)
        pe.sem_inc(pe_done, 1)
        with pe.Fori(0, PAIRS - 1) as j:
            pair(j)
        pair(PAIRS - 1, last=True)

        for _ in first_out:
            pass
        for _ in dense(1, KT, Q_OUT + 4, T_OUT + 1, act_hi, act_lo, operand=y_operand):
            pass
        with pe.Fori(1, KT // 2) as i:
            for _ in dense(2, KT, Q_OUT, T_OUT, act_hi, act_lo, 8, 2, i):
                pass

        def up(first, count, g):
            for _ in dense(count, KT, Q_MLP + 4 * first, T_MLP + first, act_hi, act_lo, 64, 24, g,
                           operand=lambda k: pe.wait_ge(act_ready, KT + k + 1)):
                pass

        def down(g):
            return dense(KT, UT, Q_MLP + 4 * UT, T_MLP + UT, u_hi, u_lo, 64, 24, g,
                         operand=lambda k: pe.wait_ge(u_ready, at(k + 1, UT, g)))

        up(0, 1, 0)
        pe.wait_ge(acc_step, ACC_STEPS)
        for a in range(2):
            M(PW[:, a, 0:HALF], ones[:], acc[:, a * HALF:(a + 1) * HALF], start=True, stop=False)
        pe.wait_ge(last_squared, 1)
        for a in range(2):
            ins = M(PW[:, a, 0:HALF], ones[:], sq_last[:, a * HALF:(a + 1) * HALF], start=False, stop=True)
        ins.then_inc(summed, 1)
        with pe.Fori(0, FFG - 1) as g:
            up(1, UT - 1, g)
            for _ in down(g):
                pass
            up(0, 1, g + 1)
        up(1, UT - 1, FFG - 1)

        def turn_out(m):
            pe.wait_ge(gained, m + 1)
            if m >= 4:
                pe.wait_ge(fin_kept, m - 3)
            for t in range(4):
                ins = nc.tensor.transpose(PW[:, m % 4, t * P:(t + 1) * P],
                                          nt1[:, m % 3, META + t * P:META + (t + 1) * P], ident[:])
            ins.then_inc(fin_turned, 1)

        pe.wait_ge(rooted, 1)
        for i, _ in enumerate(down(FFG - 1), 1):
            if i % UT == 0 and i > UT:
                turn_out(i // UT - 2)
        pe.wait_ge(acc_step, 2 * ACC_STEPS)
        pe.wait_ge(fin_kept, KT - 3)
        turn_out(KT - 1)
        pe.wait_ge(last_squared, 2)
        for t in range(4):
            for i, squares in enumerate((acc, sq_last)):
                ins = M(PW[:, 0, t:t + 1], squares[:, META + t * P:META + (t + 1) * P], ones[:, 0:1], start=(i == 0),
                        stop=(i == 1))
        ins.then_inc(summed, 1)

    ctx.close()


_INS = ["x", "meta_tokens", "norm_mix_g", "w_in", "shift_mu", "conv_w", "decay_w0", "decay_w2", "iclr_a0",
        "iclr_a2", "gate_g2", "k_k", "k_a", "r_k", "lnx_w", "lnx_b", "w_out", "norm_mlp_g", "w_up", "w_down",
        "final_norm_g"]


def kernel(**inputs):
    import numpy as _np
    import concourse.bacc as _bacc
    from concourse.bass_utils import run_bass_kernel_spmd as _run

    nc = _bacc.Bacc("TRN2", target_bir_lowering=False, num_devices=1)
    arrays, args = {}, []
    for name in _INS:
        a = _np.ascontiguousarray(inputs[name])
        if name not in ("meta_tokens", "final_norm_g"):
            a = a[0]
        if name == "r_k":
            a = a.reshape(-1)
        arrays[f"in_{name}"] = a
        args.append(nc.dram_tensor(f"in_{name}", a.shape, mybir.dt.from_np(a.dtype), kind="ExternalInput").ap())
    args.append(nc.dram_tensor("out_0", (SEQ, D), F32, kind="ExternalOutput").ap())
    hybrid_layer(nc, *args)
    r = _run(nc, [arrays], core_ids=[0])
    return r.results[0]["out_0"].reshape(1, SEQ, D)
```
